# Optimizing a Trainium2 kernel written in Bass

```python
import math
import jax, jax.numpy as jnp
from jax import lax
import numpy as np

D_MODEL = 1024
BATCH = 1
SEQ = 512
DEPTH = 2

D_FF = ((8 * D_MODEL // 3 + 127) // 128) * 128
D_CONV = D_MODEL
CONV_WIDTH = 31
CONV_GROUPS = 8
D_RNN = ((4 * D_MODEL // 3 + 127) // 128) * 128
RNN_BLOCKS = 16
RNN_BLOCK = D_RNN // RNN_BLOCKS
RNN_CONV_WIDTH = 4
RG_LRU_C = 8.0
LN_EPS = 1e-5
D_IN = 2 * D_CONV + 2 * D_RNN + 2 * D_MODEL
SPLITS = [D_CONV, 2 * D_CONV, 2 * D_CONV + D_RNN, 2 * D_CONV + 2 * D_RNN, 2 * D_CONV + 2 * D_RNN + D_MODEL]
DEEPNORM_ALPHA = (2 * DEPTH) ** 0.25
DEEPNORM_BETA = (8 * DEPTH) ** -0.25

kernel_name = "hybrid_conformer_conv_rglru_deepnorm"

def layer_norm(x, g, b):
    xf = x.astype(jnp.float32)
    mu = jnp.mean(xf, axis=-1, keepdims=True)
    xc = xf - mu
    var = jnp.mean(xc * xc, axis=-1, keepdims=True)
    y = xc * lax.rsqrt(var + LN_EPS) * g.astype(jnp.float32) + b.astype(jnp.float32)
    return y.astype(x.dtype)

def group_norm(x, g, b, groups):
    B, S, C = x.shape
    xf = x.astype(jnp.float32).reshape(B, S, groups, C // groups)
    mu = jnp.mean(xf, axis=-1, keepdims=True)
    xc = xf - mu
    var = jnp.mean(xc * xc, axis=-1, keepdims=True)
    y = (xc * lax.rsqrt(var + LN_EPS)).reshape(B, S, C)
    y = y * g.astype(jnp.float32) + b.astype(jnp.float32)
    return y.astype(x.dtype)

def swiglu_ffn(x, w_gu, w_down):
    gate, up = jnp.split(x @ w_gu, 2, axis=-1)
    return (jax.nn.silu(gate) * up) @ w_down

def causal_depthwise_conv(x, w, b):
    K, C = w.shape
    y = lax.conv_general_dilated(
        x, w[:, None, :].astype(x.dtype),
        window_strides=(1,), padding=[(K - 1, 0)],
        dimension_numbers=("NWC", "WIO", "NWC"),
        feature_group_count=C)
    return y + b

def block_diag_linear(x, w, b):
    B, S, _ = x.shape
    xh = x.reshape(B, S, RNN_BLOCKS, RNN_BLOCK)
    y = jnp.einsum("bshi,hij->bshj", xh, w)
    return y.reshape(B, S, D_RNN) + b

def rg_lru(x, w_a, b_a, w_x, b_x, lam):
    r = jax.nn.sigmoid(block_diag_linear(x, w_a, b_a)).astype(jnp.float32)
    i = jax.nn.sigmoid(block_diag_linear(x, w_x, b_x)).astype(jnp.float32)
    log_a = -RG_LRU_C * r * jax.nn.softplus(-lam.astype(jnp.float32))
    a = jnp.exp(log_a)
    mult = jnp.sqrt(-jnp.expm1(2.0 * log_a))
    u = mult * (i * x.astype(jnp.float32))

    def combine(left, right):
        a1, b1 = left
        a2, b2 = right
        return a1 * a2, a2 * b1 + b2

    _, h = lax.associative_scan(combine, (a, u), axis=1)
    return h.astype(x.dtype)

def hybrid_mixer(x, w_in, b_in, dw_w, dw_b, gn_g, gn_b, conv_w_proj,
                 rc_w, rc_b, w_a, b_a, w_x, b_x, lam, rnn_w_proj, w_out):
    u = x @ w_in + b_in
    c_val, c_gate, r_x, r_gate, g_c, g_r = jnp.split(u, SPLITS, axis=-1)
    c = c_val * jax.nn.sigmoid(c_gate)
    c = causal_depthwise_conv(c, dw_w, dw_b)
    c = jax.nn.silu(group_norm(c, gn_g, gn_b, CONV_GROUPS))
    y_conv = c @ conv_w_proj
    r = causal_depthwise_conv(r_x, rc_w, rc_b)
    h = rg_lru(r, w_a, b_a, w_x, b_x, lam)
    y_rnn = (h * jax.nn.gelu(r_gate)) @ rnn_w_proj
    m = jax.nn.sigmoid(g_c) * y_conv + jax.nn.sigmoid(g_r) * y_rnn
    return m @ w_out

def setup_inputs(seed: int = 0) -> dict:
    key = jax.random.key(seed)
    ks = jax.random.split(key, 32)
    L = DEPTH
    f32 = jnp.float32

    def nrm(k, shape, scale):
        return jax.random.normal(k, shape, f32) * scale

    def gain(k, shape):
        return 1.0 + nrm(k, shape, 0.02)

    u = jax.random.uniform(ks[18], (L, D_RNN), f32, minval=0.9, maxval=0.999)
    log_a = jnp.log(u) / RG_LRU_C
    lam = log_a - jnp.log(-jnp.expm1(log_a))

    return {
        "x": nrm(ks[0], (BATCH, SEQ, D_MODEL), 1.0),
        "ffn1_w_gu": nrm(ks[1], (L, D_MODEL, 2 * D_FF), D_MODEL ** -0.5),
        "ffn1_w_down": nrm(ks[2], (L, D_FF, D_MODEL), DEEPNORM_BETA * D_FF ** -0.5),
        "ln1_g": gain(ks[3], (L, D_MODEL)),
        "ln1_b": nrm(ks[4], (L, D_MODEL), 0.02),
        "mix_w_in": nrm(ks[5], (L, D_MODEL, D_IN), D_MODEL ** -0.5),
        "mix_b_in": nrm(ks[6], (L, D_IN), 0.02),
        "conv_dw_w": nrm(ks[7], (L, CONV_WIDTH, D_CONV), CONV_WIDTH ** -0.5),
        "conv_dw_b": nrm(ks[8], (L, D_CONV), 0.02),
        "conv_gn_g": gain(ks[9], (L, D_CONV)),
        "conv_gn_b": nrm(ks[10], (L, D_CONV), 0.02),
        "conv_w_proj": nrm(ks[11], (L, D_CONV, D_MODEL), DEEPNORM_BETA * D_CONV ** -0.5),
        "rnn_conv_w": nrm(ks[12], (L, RNN_CONV_WIDTH, D_RNN), RNN_CONV_WIDTH ** -0.5),
        "rnn_conv_b": nrm(ks[13], (L, D_RNN), 0.02),
        "rnn_w_a": nrm(ks[14], (L, RNN_BLOCKS, RNN_BLOCK, RNN_BLOCK), RNN_BLOCK ** -0.5),
        "rnn_b_a": nrm(ks[15], (L, D_RNN), 0.02),
        "rnn_w_x": nrm(ks[16], (L, RNN_BLOCKS, RNN_BLOCK, RNN_BLOCK), RNN_BLOCK ** -0.5),
        "rnn_b_x": nrm(ks[17], (L, D_RNN), 0.02),
        "rnn_lambda": lam,
        "rnn_w_proj": nrm(ks[19], (L, D_RNN, D_MODEL), DEEPNORM_BETA * D_RNN ** -0.5),
        "mix_w_out": nrm(ks[20], (L, D_MODEL, D_MODEL), DEEPNORM_BETA * D_MODEL ** -0.5),
        "ln2_g": gain(ks[21], (L, D_MODEL)),
        "ln2_b": nrm(ks[22], (L, D_MODEL), 0.02),
        "ffn2_w_gu": nrm(ks[23], (L, D_MODEL, 2 * D_FF), D_MODEL ** -0.5),
        "ffn2_w_down": nrm(ks[24], (L, D_FF, D_MODEL), DEEPNORM_BETA * D_FF ** -0.5),
        "ln3_g": gain(ks[25], (L, D_MODEL)),
        "ln3_b": nrm(ks[26], (L, D_MODEL), 0.02),
    }

def reference(x, ffn1_w_gu, ffn1_w_down, ln1_g, ln1_b, mix_w_in, mix_b_in,
              conv_dw_w, conv_dw_b, conv_gn_g, conv_gn_b, conv_w_proj,
              rnn_conv_w, rnn_conv_b, rnn_w_a, rnn_b_a, rnn_w_x, rnn_b_x,
              rnn_lambda, rnn_w_proj, mix_w_out, ln2_g, ln2_b,
              ffn2_w_gu, ffn2_w_down, ln3_g, ln3_b):
    for l in range(DEPTH):
        x = layer_norm(DEEPNORM_ALPHA * x + 0.5 * swiglu_ffn(x, ffn1_w_gu[l], ffn1_w_down[l]),
                       ln1_g[l], ln1_b[l])
        mix = hybrid_mixer(x, mix_w_in[l], mix_b_in[l], conv_dw_w[l], conv_dw_b[l],
                           conv_gn_g[l], conv_gn_b[l], conv_w_proj[l],
                           rnn_conv_w[l], rnn_conv_b[l], rnn_w_a[l], rnn_b_a[l],
                           rnn_w_x[l], rnn_b_x[l], rnn_lambda[l], rnn_w_proj[l], mix_w_out[l])
        x = layer_norm(DEEPNORM_ALPHA * x + mix, ln2_g[l], ln2_b[l])
        x = layer_norm(DEEPNORM_ALPHA * x + 0.5 * swiglu_ffn(x, ffn2_w_gu[l], ffn2_w_down[l]),
                       ln3_g[l], ln3_b[l])
    return x


_drawn_inputs = setup_inputs


def setup_inputs(seed=0):
    import zlib

    import numpy as np

    out = dict(_drawn_inputs(seed))
    spreads = {}
    factors = {'mix_b_in': 6.75,
     'conv_dw_b': 8.0,
     'conv_gn_g': 32.79,
     'conv_gn_b': 33.72,
     'rnn_conv_b': 56.048,
     'rnn_w_a': 28.472,
     'rnn_b_a': 64.0,
     'rnn_b_x': 64.0,
     'rnn_lambda': 25.448,
     'rnn_conv_w': 8.0,
     'rnn_w_x': 8.0,
     'rnn_w_proj': 8.0}
    for name, (base, spread) in spreads.items():
        noise = np.random.default_rng([zlib.crc32(name.encode()), seed]).standard_normal(out[name].shape)
        drawn = base * np.exp(spread * noise) if base else spread * noise
        out[name] = __import__('jax').numpy.asarray(drawn.astype(out[name].dtype))
    for name, factor in factors.items():
        out[name] = (out[name] * factor).astype(out[name].dtype)
    return out
```

```python
import math

import concourse.bass as bass
from concourse import mybir

F32 = mybir.dt.float32
F32R = mybir.dt.float32r
ALU = mybir.AluOpType
ACT = mybir.ActivationFunctionType

P = 128
RING = 4
AHEAD = 3
EPS = 1e-5

L, S, D = 2, 512, 1024
DFF, DRNN = 2816, 1408
TAPS, RTAPS = 31, 4
KD, KF, KR = D // P, DFF // P, DRNN // P
NB = S // P
RB = DRNN // 16
ALPHA = (2 * L) ** 0.25
UW = 1024

FFN_UNITS = 2 * KF + KF
U_FFN = (0, 0)
MIX = FFN_UNITS
U_C, U_RG = MIX, MIX + 2 * KD
U_R = U_RG + KR
U_G = U_R + 3 * KR
U_Y = U_G + 2 * KD
U_O = U_Y + 3 * KD
U_FFN = (0, U_O + KD)
UPL = U_FFN[1] + FFN_UNITS
assert UPL % RING == 0

R_UNITS = [("rx", 0), ("rx", 1)]
for _j in range(KR):
    if _j + 2 < KR:
        R_UNITS.append(("rx", _j + 2))
    R_UNITS += [("bda", _j), ("bdx", _j)]
assert len(R_UNITS) == 3 * KR
Y_SPLIT = [(0, 7), (7, 13), (13, KD + KR)]

PC = {}
_n = 0
for _name, _w in (("b_c", 2 * KD), ("b_rg", KR), ("b_rx", KR), ("b_g", 2 * KD), ("cw", KD * TAPS), ("cb", KD),
                  ("gg", KD), ("gb", KD), ("rw", KR * RTAPS), ("rb", KR), ("ba", KR), ("bx", KR), ("lam", KR)):
    PC[_name] = _n
    _n += _w
NPAR = _n
SQ_UP = 2.0 ** 60


def adv(q, s, d):
    return q + (s + d) // RING, (s + d) % RING


def trunk(nc, wst, xT, xtok, par, lnp, out):
    sb, at = nc.alloc_sbuf_tensor, nc.alloc_sbuf_tensor_at
    w_raw = sb("w_raw", [P, RING, UW], F32)
    w_hi = sb("w_hi", [P, RING, UW], F32R)
    w_lo = sb("w_lo", [P, RING, UW], F32R)
    x_hi = sb("x_hi", [P, KD, S], F32R)
    x_lo = sb("x_lo", [P, KD, S], F32R)
    res = sb("res", [P, NB, D], F32)
    a_hi = sb("a_hi", [P, RING, S], F32R)
    a_lo = sb("a_lo", [P, RING, S], F32R)
    pr = sb("pr", [P, L * NPAR], F32)
    sp8 = sb("sp8", [P, 2, L * KR], F32)
    lt = sb("lt", [P, 4, L * KR], F32)
    ident = sb("ident", [P, P], F32)
    avg = sb("avg", [P, P], F32)
    lns = sb("lns", [P, 2, 20], F32)
    mhalf = sb("mhalf", [P, 1], F32)

    arena = sb("arena", [P, 23040], F32)
    A0 = nc.sbuf_base - 23040 * 4
    gates = at("gates", [P, 2 * KD, S], F32, offset=A0)
    hgm = at("hgm", [P, KR, S], F32, offset=A0 + 32768)
    cpad = at("cpad", [P, KD, TAPS - 1 + S], F32, offset=A0 + 55296)
    ct = at("ct", [P, 6, S], F32, offset=A0 + 72640)
    rxp = at("rxp", [P, 2, RTAPS - 1 + S], F32, offset=A0 + 84928)
    tx = at("tx", [P, 1, S], F32, offset=A0 + 89056)
    hg_hi = at("hg_hi", [P, 9, S], F32R, offset=A0 + 55296)
    hg_lo = at("hg_lo", [P, 9, S], F32R, offset=A0 + 55296 + 18432)
    h = at("h", [P, KF, S], F32, offset=A0)
    sg = at("sg", [P, 1, S], F32, offset=A0 + 45056)
    yb = at("yb", [P, 2, D], F32, offset=A0 + 47104)
    gb = at("gb", [P, 2, D], F32, offset=A0 + 55296)

    acc0, acc1, gx, gsq, grs, gy = (ct[:, i] for i in range(6))
    sgc = tx[:, 0]
    rcf = [gates[:, 11 + i] for i in range(4)]
    RT = [[gates[:, 15], tx[:, 0], ct[:, 0], ct[:, 1]], [ct[:, 2], ct[:, 3], ct[:, 4], ct[:, 5]]]

    bank = [nc.alloc_psum_tensor(f"bank{i}", [P, S], F32) for i in range(8)]

    sem = nc.alloc_semaphore
    raw_landed = [sem(f"raw_landed{i}") for i in range(RING)]
    x_landed, res_landed, par_landed, gb_landed = sem("x_landed"), sem("res_landed"), sem("par_landed"), sem("gb_landed")
    out_written = sem("out_written")
    consts, eps_ready = sem("consts"), sem("eps_ready")
    settled = sem("settled")
    hi_ready, lo_ready, unit_done = sem("hi_ready"), sem("lo_ready"), sem("unit_done")
    lam_act, lam_dve = sem("lam_act"), sem("lam_dve")
    silu_done, hmul_done = sem("silu_done"), sem("hmul_done")
    ahi_ready, alo_ready = sem("ahi_ready"), sem("alo_ready")
    blk_done, ln_chain, rstd_ready, y_ready = sem("blk_done"), sem("ln_chain"), sem("rstd_ready"), sem("y_ready")
    xpose_done, xhi_ready, xlo_ready = sem("xpose_done"), sem("xhi_ready"), sem("xlo_ready")
    pads_ready = sem("pads_ready")
    csig_done, cmul_done = sem("csig_done"), sem("cmul_done")
    tap_done, conv_done = sem("tap_done"), sem("conv_done")
    mean_done, xc_done, sq_done, var_done = sem("mean_done"), sem("xc_done"), sem("sq_done"), sem("var_done")
    gln_done, grs_done, gy_done, gn_done = sem("gln_done"), sem("grs_done"), sem("gy_done"), sem("gn_done")
    gelu_done, rx_done, rtap_done, rc_done = sem("gelu_done"), sem("rx_done"), sem("rtap_done"), sem("rc_done")
    rchi_ready, rclo_ready = sem("rchi_ready"), sem("rclo_ready")
    ra_done, rs_done, rv_done, ru_done, hg_done = (sem(x) for x in ("ra_done", "rs_done", "rv_done", "ru_done", "hg_done"))
    gate_done = sem("gate_done")
    cs_hi, cs_lo, hs_hi, hs_lo = (sem(x) for x in ("cs_hi", "cs_lo", "hs_hi", "hs_lo"))
    mm_done, m_done = sem("mm_done"), sem("m_done")

    C_HMUL, C_CMUL, C_GELU, C_RX, C_RA, C_GATE, C_M, C_Y = 2, 2, 4, 2, 2, 4, 2, NB

    def U(q, s):
        return q * RING + s

    def q0(l, rel):
        return l * (UPL // RING) + rel // RING, rel % RING

    def one(t, i):
        return t[:, bass.ds(i, 1)].rearrange("p a n -> p (a n)")

    def col(name, l, i):
        return pr[:, bass.ds(l * NPAR + (i + PC[name]), 1)]

    def f32(ap):
        return ap.bitcast(F32)

    def settle(eng):
        eng.sem_inc(settled, 1)

    with nc.Block() as block:

        @block.sync
        def _(sp):
            def load(q, s, cols=UW):
                sp.wait_ge(lo_ready, U(q, s) + 1)
                sp.dma_start(w_raw[:, s, 0:cols],
                             wst[bass.ds(U(q, s), 1), :, 0:cols].rearrange("u p n -> (u p) n")
                             ).then_inc(raw_landed[s], 16)

            def loads(q, s, n):
                with sp.Fori(0, n // RING) as it:
                    for i in range(RING):
                        load(*adv(q + it, s, i))
                for i in range(n // RING * RING, n):
                    load(*adv(q, s, i))

            sp.dma_start(h[:, 0:KD // 2], xT[:, 0:KD // 2]).then_inc(x_landed, 16)
            sp.dma_start(h[:, KD // 2:KD], xT[:, KD // 2:KD]).then_inc(x_landed, 16)
            with sp.Fori(0, L) as l:
                loads(*q0(l, 0), U_R)
                for i, (kind, _) in enumerate(R_UNITS):
                    load(*q0(l, U_R + i), UW if kind == "rx" else 3 * P)
                loads(*q0(l, U_G), 2 * KD)
                with sp.Fori(0, 2) as yi:
                    qy, sy = q0(l, U_Y)
                    for i in range(12):
                        k0, k1 = Y_SPLIT[i % 3]
                        load(*adv(qy + yi * 3, sy, i), (k1 - k0) * P)
                loads(*q0(l, U_O), UPL - U_O)
            for s in range(AHEAD):
                sp.wait_ge(lo_ready, L * UPL + s + 1)
                sp.dma_start(w_raw[:, s], wst[s]).then_inc(raw_landed[s], 16)
            sp.wait_ge(y_ready, C_Y + L * 3 * NB)
            sp.dma_start(out.rearrange("(b p) d -> p b d", p=P), res[:]).then_inc(out_written, 16)
            sp.wait_ge(out_written, 16)

        @block.gpsimd
        def _(pool):
            pool.sem_inc(y_ready, C_Y)
            pool.dma_start(pr[:], par).then_inc(par_landed, 16)
            pool.dma_start(res[:], xtok.rearrange("(b p) d -> p b d", p=P)).then_inc(res_landed, 16)
            pool.memset(ident[:], 0.0).then_inc(consts, 1)
            pool.memset(avg[:], 1.0 / P).then_inc(consts, 1)
            pool.memset(mhalf[:], -0.5).then_inc(consts, 1)
            pool.wait_ge(consts, 3)
            pool.affine_select(out=ident[:], in_=ident[:], compare_op=ALU.not_equal, fill=1.0, base=0,
                               pattern=[[-1, P]], channel_multiplier=1).then_inc(consts, 1)
            pool.wait_ge(consts, 4)

            def layer_norm(l, n, ready):
                ready()
                pool.dma_start(gb[:], lnp[bass.ds(l * 3 + n, 1)].rearrange("a p c d -> p (a c) d")
                               ).then_inc(gb_landed, 16)
                for b in range(NB):
                    X = l * 12 + (4 * n + b)
                    if b >= 2:
                        pool.wait_ge(y_ready, X + (C_Y - 1))
                    pool.wait_ge(ln_chain, X * 7 + 6)
                    pool.tensor_tensor(lns[:, b % 2, 16:17], lns[:, b % 2, 15:16], mhalf[:], ALU.pow
                                       ).then_inc(rstd_ready, 1)

            with pool.Fori(0, L) as l:
                layer_norm(l, 0, lambda: pool.wait_ge(y_ready, l * 12 + C_Y))
                pool.wait_ge(y_ready, l * 12 + (C_Y + 4))
                settle(pool)
                pool.memset(cpad[:, :, 0:TAPS - 1], 0.0).then_inc(pads_ready, 1)
                pool.memset(rxp[:, :, 0:RTAPS - 1], 0.0).then_inc(pads_ready, 1)
                layer_norm(l, 1, lambda: pool.wait_ge(unit_done, l * UPL + (U_O + RING)))
                layer_norm(l, 2, lambda: pool.wait_ge(y_ready, l * 12 + (C_Y + 8)))

        @block.scalar
        def _(act):
            act.sem_inc(gelu_done, C_GELU)
            act.sem_inc(rx_done, C_RX)
            act.sem_inc(ra_done, C_RA * 5)
            act.sem_inc(gate_done, C_GATE)

            def split(q, s, cols=UW):
                act.wait_ge(raw_landed[s], q * 16 + 16)
                act.wait_ge(unit_done, U(q, s) + 1)
                act.activation(w_hi[:, s, 0:cols], w_raw[:, s, 0:cols], ACT.Copy).then_inc(hi_ready, 1)

            def asplit(q, s, src, k, n):
                act.wait_ge(unit_done, U(q, s) + 1)
                act.activation(a_hi[:, s], one(src, k), ACT.Copy).then_inc(ahi_ready, 1)

            def xt(l, n, b):
                for i in range(2):
                    act.wait_ge(xpose_done, l * 24 + (8 * n + 2 * b + i + 1))
                    act.activation(x_hi[:, 4 * i:4 * i + 4, b * P:(b + 1) * P],
                                   bank[2 * b + i][:].rearrange("p (k n) -> p k n", k=4), ACT.Copy
                                   ).then_inc(xhi_ready, 1)

            def tail(l, n, q, s):
                xt(l, n, 0)
                split(*adv(q, s, 0))
                xt(l, n, 1)
                xt(l, n, 2)
                split(*adv(q, s, 1))
                xt(l, n, 3)
                split(*adv(q, s, 2))

            def ffn(l, f):
                q, s = q0(l, U_FFN[f])

                def pair(q, s, t, down):
                    T = l * (2 * KF) + (f * KF + t)
                    for i in range(2):
                        split(*adv(q, s, AHEAD + i))
                        if down[i] is not None:
                            asplit(*adv(q, s, AHEAD + i), h, down[i], None)
                    act.wait_ge(unit_done, U(q, s) + (RING + 1))
                    act.wait_ge(hmul_done, T + C_HMUL)
                    act.activation(sg[:, 0], bank[down[2]][:], ACT.Silu).then_inc(silu_done, 1)

                with act.Fori(0, KF // 2 - 1) as it:
                    pair(*adv(q + it, s, 0), it * 2, (None, None, 0))
                    pair(*adv(q + it, s, 2), it * 2 + 1, (None, None, 2))
                pair(*adv(q, s, 2 * KF - 4), KF - 2, (None, 0, 0))
                pair(*adv(q, s, 2 * KF - 2), KF - 1, (1, 2, 2))
                qd, sd = adv(q, s, 2 * KF)
                for k in (0, 1):
                    split(*adv(qd, sd, k + AHEAD))
                    asplit(*adv(qd, sd, k + AHEAD), h, k + AHEAD, None)
                with act.Fori(0, 4) as it:
                    for i in range(4):
                        split(*adv(qd + it, sd, 2 + i + AHEAD))
                        asplit(*adv(qd + it, sd, 2 + i + AHEAD), h, it * 4 + (2 + i + AHEAD), None)
                split(*adv(qd, sd, 18 + AHEAD))
                asplit(*adv(qd, sd, 18 + AHEAD), h, 18 + AHEAD, None)
                tail(l, 2 * f, *adv(qd, sd, KF))

            def gn_square(l, g):
                act.wait_ge(xc_done, l * KD + g + 1)
                act.activation(gsq, gx, ACT.Square).then_inc(sq_done, 1)

            def gn_finish(l, g):
                act.wait_ge(var_done, l * KD + g + 1)
                act.activation(gsq, bank[7][:], ACT.Ln, bias=epsb[:, 0:1]).then_inc(gln_done, 1)
                act.wait_ge(gln_done, l * KD + g + 1)
                act.activation(grs, gsq, ACT.Exp, scale=-0.5).then_inc(grs_done, 1)
                act.wait_ge(gy_done, l * KD + g + 1)
                act.activation(one(cpad, g)[:, TAPS - 1:] if isinstance(g, int) else
                               cpad[:, bass.ds(g, 1), TAPS - 1:].rearrange("p a n -> p (a n)"),
                               gy, ACT.Silu, bias=col("gb", l, g), scale=col("gg", l, g)).then_inc(gn_done, 1)

            def group(l, q, s, post, g, n=4):
                for i in range(n):
                    split(*adv(q, s, i + AHEAD))
                    if i > 0:
                        post(i - 1)
                    if i == 2 and g is not None:
                        gn_square(l, g)
                post(n - 1)
                if g is not None:
                    gn_finish(l, g)

            epsb = lns[:, 0, 18:19]
            act.wait_ge(eps_ready, 1)
            act.wait_ge(x_landed, 32)
            for k in range(KD):
                act.activation(x_hi[:, k], h[:, k], ACT.Copy).then_inc(xhi_ready, 1)
            for s in range(AHEAD):
                act.wait_ge(raw_landed[s], 16)
                act.activation(w_hi[:, s], w_raw[:, s], ACT.Copy).then_inc(hi_ready, 1)
            act.wait_ge(lam_dve, 1)
            act.activation(lt[:, 1], lt[:, 0], ACT.Exp, scale=-1.0).then_inc(lam_act, 1)

            with act.Fori(0, L) as l:
                ffn(l, 0)

                def c_group(it, g):
                    q, s = q0(l, U_C)

                    def post(i):
                        if i % 2:
                            j = it * 2 + i // 2
                            act.wait_ge(unit_done, U(*adv(q + it, s, i)) + (RING + 1))
                            act.wait_ge(cmul_done, l * KD + j + C_CMUL)
                            act.activation(sgc, bank[2 * (i // 2) + 1][:], ACT.Sigmoid,
                                           bias=col("b_c", l, j * 2 + 1)).then_inc(csig_done, 1)
                    group(l, q + it, s, post, g)

                c_group(0, None)
                c_group(1, None)
                with act.Fori(2, 4) as it:
                    c_group(it, it - 2)

                def rg_group(it, g, n=4):
                    q, s = q0(l, U_RG)

                    def post(i):
                        act.wait_ge(unit_done, U(*adv(q + it, s, i)) + (RING + 1))
                        act.activation(one(gates, it * 4 + i), bank[i][:], ACT.Gelu_apprx_tanh,
                                       bias=col("b_rg", l, it * 4 + i)).then_inc(gelu_done, 1)
                    group(l, q + it, s, post, g, n) if n == 4 else rg_last(q + it, s, post, g)

                def rg_last(q, s, post, g):
                    for i in range(3):
                        kind = R_UNITS[i][0]
                        split(*adv(q, s, i + AHEAD), UW if kind == "rx" else 3 * P)
                        if i > 0:
                            post(i - 1)
                        if i == 2:
                            gn_square(l, g)
                    post(2)
                    gn_finish(l, g)

                with act.Fori(0, 2) as it:
                    rg_group(it, it + 2)
                rg_group(2, 4, 3)

                def rx_evac(j):
                    act.wait_ge(unit_done, l * UPL + (U_R + R_UNITS.index(("rx", j)) + RING + 1))
                    act.wait_ge(pads_ready, l * 2 + 2)
                    if j >= 2:
                        act.wait_ge(rc_done, l * KR + (j - 1))
                    act.activation(rxp[:, j % 2, RTAPS - 1:], bank[4 + j % 2][:], ACT.Identity,
                                   bias=col("b_rx", l, j)).then_inc(rx_done, 1)

                def rc_hi(j):
                    act.wait_ge(rc_done, l * KR + (j + 1))
                    if j >= 4:
                        act.wait_ge(unit_done, l * UPL + (U_R + R_UNITS.index(("bdx", j - 3)) + RING + 1))
                    act.activation(a_hi[:, j % 4], rcf[j % 4], ACT.Copy).then_inc(rchi_ready, 1)

                def r_stage_a(j):
                    r, i, a, v = RT[j % 2]
                    n = l * (KR * 5) + (5 * j + C_RA * 5)
                    act.wait_ge(unit_done, l * UPL + (U_R + R_UNITS.index(("bdx", j)) + RING + 1))
                    if j >= 2:
                        act.wait_ge(hg_done, l * KR + (j - 1))
                    act.activation(r, bank[j % 2][:], ACT.Sigmoid, bias=col("ba", l, j)).then_inc(ra_done, 1)
                    act.activation(i, bank[2 + j % 2][:], ACT.Sigmoid, bias=col("bx", l, j)).then_inc(ra_done, 1)
                    act.wait_ge(ra_done, n + 2)
                    act.activation(a, r, ACT.Exp, scale=sp8[:, 1, bass.ds(l * KR + j, 1)]).then_inc(ra_done, 1)
                    act.wait_ge(ra_done, n + 3)
                    act.activation(v, a, ACT.Square).then_inc(ra_done, 1)
                    act.activation(r, r, ACT.Tanh, scale=sp8[:, 0, bass.ds(l * KR + j, 1)]).then_inc(ra_done, 1)

                def r_stage_b(j):
                    v = RT[j % 2][3]
                    act.wait_ge(rv_done, l * (KR * 2) + (2 * j + 2))
                    act.activation(v, v, ACT.Sqrt, scale=SQ_UP).then_inc(rs_done, 1)

                for i, (kind, j) in enumerate(R_UNITS):
                    n = i + AHEAD
                    ahead = R_UNITS[n][0] if n < len(R_UNITS) else "g"
                    split(*q0(l, U_R + n), 3 * P if ahead.startswith("bd") else UW)
                    if i >= 2 and R_UNITS[i - 2][0] == "rx":
                        rc_hi(R_UNITS[i - 2][1])
                    if i >= 1:
                        pk, pj = R_UNITS[i - 1]
                        if pk == "rx":
                            rx_evac(pj)
                        elif pk == "bdx":
                            r_stage_a(pj)
                        elif pk == "bda" and pj >= 1:
                            r_stage_b(pj - 1)
                r_stage_a(KR - 1)
                r_stage_b(KR - 1)

                def g_group(it, g, last=False):
                    q, s = q0(l, U_G)

                    def post(i):
                        act.wait_ge(unit_done, U(*adv(q + it, s, i)) + (RING + 1))
                        act.activation(one(gates, it * 4 + i), bank[i][:], ACT.Sigmoid,
                                       bias=col("b_g", l, it * 4 + i)).then_inc(gate_done, 1)
                    if not last:
                        group(l, q + it, s, post, g)
                        return
                    for i in range(4):
                        k0, k1 = Y_SPLIT[(i - 1) % 3]
                        split(*adv(q + it, s, i + AHEAD), UW if i == 0 else (k1 - k0) * P)
                        if i > 0:
                            post(i - 1)
                        if i == 2:
                            gn_square(l, g)
                    post(3)
                    gn_finish(l, g)

                act.wait_ge(hg_done, l * KR + KR)
                g_group(0, None)
                with act.Fori(1, 3) as it:
                    g_group(it, it + 4)
                g_group(3, 7, last=True)

                act.wait_ge(unit_done, l * UPL + (U_Y + RING))
                act.wait_ge(gn_done, l * KD + KD)
                for j in range(KD):
                    act.activation(x_hi[:, j], cpad[:, j, TAPS - 1:], ACT.Copy).then_inc(cs_hi, 1)
                act.wait_ge(cs_lo, l * KD + KD)
                for j in range(KR):
                    dst = hg_hi[:, j] if j < 9 else a_hi[:, j - 9]
                    act.activation(dst, hgm[:, j], ACT.Copy).then_inc(hs_hi, 1)
                for i in range(3 * KD):
                    n = i + AHEAD
                    if n < 3 * KD:
                        k0, k1 = Y_SPLIT[n % 3]
                        split(*q0(l, U_Y + n), (k1 - k0) * P)
                    else:
                        split(*q0(l, U_Y + n))
                        if n < 3 * KD + 2:
                            act.wait_ge(m_done, l * KD + (n - 3 * KD + 1 + C_M))
                            asplit(*q0(l, U_Y + n), hgm, n - 3 * KD, None)

                act.wait_ge(unit_done, l * UPL + (U_O + RING))
                asplit(*q0(l, U_O + 2), hgm, 2, None)
                for k in range(KD - AHEAD):
                    split(*q0(l, U_O + k + AHEAD))
                    act.wait_ge(m_done, l * KD + (k + AHEAD + 1 + C_M))
                    asplit(*q0(l, U_O + k + AHEAD), hgm, k + AHEAD, None)
                tail(l, 1, *q0(l, U_O + KD))

                ffn(l, 1)

        @block.vector
        def _(dve):
            dve.sem_inc(lo_ready, RING)
            dve.sem_inc(hmul_done, C_HMUL)
            dve.sem_inc(cmul_done, C_CMUL)
            dve.sem_inc(m_done, C_M)

            def split(q, s, cols=UW):
                dve.wait_ge(hi_ready, U(q, s) + 1)
                dve.tensor_tensor(w_lo[:, s, 0:cols], w_raw[:, s, 0:cols], f32(w_hi[:, s, 0:cols]),
                                  ALU.subtract).then_inc(lo_ready, 1)

            def asplit(s, src, k, n):
                dve.wait_ge(ahi_ready, n + 1)
                dve.tensor_tensor(a_lo[:, s], one(src, k), f32(a_hi[:, s]), ALU.subtract).then_inc(alo_ready, 1)

            def ln(l, n, b):
                X = l * 12 + (4 * n + b)
                y, st = yb[:, b % 2], lns[:, b % 2]
                gain = (1.0 if n == 1 else 0.5) / ALPHA
                if b < NB - 1:
                    dve.wait_ge(blk_done, l * 9 + (3 * n + b + 1))
                else:
                    dve.wait_ge(unit_done, l * UPL + ((MIX, U_FFN[1], UPL)[n] + RING))
                if b >= 2:
                    dve.wait_ge(y_ready, X + (C_Y - 1))
                for i in range(2):
                    cols = slice(S * i, S * i + S)
                    dve.scalar_tensor_tensor(y[:, cols], bank[2 * b + i][:], gain, res[:, b, cols], ALU.mult, ALU.add
                                             ).then_inc(ln_chain, 1)
                for i in range(2):
                    dve.wait_ge(ln_chain, X * 7 + (i + 1))
                    dve.bn_stats(st[:, 6 * i:6 * i + 6], y[:, S * i:S * i + S]).then_inc(ln_chain, 1)
                dve.wait_ge(ln_chain, X * 7 + 4)
                settle(dve)
                dve.bn_aggr(st[:, 13:15], st[:, 0:12]).then_inc(ln_chain, 1)
                dve.wait_ge(ln_chain, X * 7 + 5)
                dve.tensor_scalar(st[:, 15:16], st[:, 14:15], EPS / ALPHA ** 2, None, ALU.add).then_inc(ln_chain, 1)
                if b == 0:
                    dve.wait_ge(gb_landed, l * 48 + (16 * n + 16))
                dve.scalar_tensor_tensor(y, y, st[:, 13:14], gb[:, 0], ALU.subtract, ALU.mult).then_inc(ln_chain, 1)
                dve.wait_ge(ln_chain, X * 7 + 7)
                dve.wait_ge(rstd_ready, X + 1)
                dve.scalar_tensor_tensor(res[:, b], y, st[:, 16:17], gb[:, 1], ALU.mult, ALU.add).then_inc(y_ready, 1)

            def xt(l, n, b):
                for i in range(2):
                    dve.wait_ge(xhi_ready, l * 24 + (KD + 8 * n + 2 * b + i + 1))
                    at = (slice(None), slice(4 * i, 4 * i + 4), slice(b * P, (b + 1) * P))
                    dve.tensor_tensor(x_lo[at], bank[2 * b + i][:].rearrange("p (k n) -> p k n", k=4),
                                      f32(x_hi[at]), ALU.subtract).then_inc(xlo_ready, 1)

            def tail(l, n, q, s):
                ln(l, n, 0)
                ln(l, n, 1)
                ln(l, n, 2)
                xt(l, n, 0)
                split(*adv(q, s, 0))
                ln(l, n, 3)
                xt(l, n, 1)
                xt(l, n, 2)
                split(*adv(q, s, 1))
                xt(l, n, 3)
                split(*adv(q, s, 2))

            def ffn(l, f):
                q, s = q0(l, U_FFN[f])
                N0 = l * (2 * KF + KD) + f * (KF + KD)

                def pair(q, s, t, down, bk):
                    T = l * (2 * KF) + (f * KF + t)
                    for i in range(2):
                        split(*adv(q, s, AHEAD + i))
                        if down[i] is not None:
                            asplit(adv(q, s, AHEAD + i)[1], h, down[i], N0 + down[i])
                    dve.wait_ge(silu_done, T + 1)
                    dve.wait_ge(unit_done, U(*adv(q, s, 1)) + (RING + 1))
                    dve.tensor_tensor(one(h, t), bank[bk + 1][:], sg[:, 0], ALU.mult).then_inc(hmul_done, 1)

                with dve.Fori(0, KF // 2 - 1) as it:
                    pair(*adv(q + it, s, 0), it * 2, (None, None), 0)
                    pair(*adv(q + it, s, 2), it * 2 + 1, (None, None), 2)
                pair(*adv(q, s, 2 * KF - 4), KF - 2, (None, 0), 0)
                pair(*adv(q, s, 2 * KF - 2), KF - 1, (1, 2), 2)
                qd, sd = adv(q, s, 2 * KF)
                for k in (0, 1):
                    split(*adv(qd, sd, k + AHEAD))
                    asplit(adv(qd, sd, k + AHEAD)[1], h, k + AHEAD, N0 + (k + AHEAD))
                with dve.Fori(0, 4) as it:
                    for i in range(4):
                        split(*adv(qd + it, sd, 2 + i + AHEAD))
                        k = it * 4 + (2 + i + AHEAD)
                        asplit(adv(qd, sd, 2 + i + AHEAD)[1], h, k, N0 + k)
                split(*adv(qd, sd, 18 + AHEAD))
                asplit(adv(qd, sd, 18 + AHEAD)[1], h, 18 + AHEAD, N0 + (18 + AHEAD))
                tail(l, 2 * f, *adv(qd, sd, KF))

            def taps(l, c, part):
                T0 = (l * KD + c) * (TAPS)
                for k in range(8 * part, min(8 * part + 8, TAPS)):
                    src = cpad[:, bass.ds(c, 1), k:k + S].rearrange("p a n -> p (a n)")
                    acc = (acc0, acc1)[k % 2]
                    w = pr[:, bass.ds(l * NPAR + c * TAPS + (PC["cw"] + k), 1)]
                    if k == 0:
                        dve.tensor_scalar(acc, src, w, col("cb", l, c), ALU.mult, ALU.add).then_inc(tap_done, 1)
                    elif k == 1:
                        dve.tensor_scalar(acc, src, w, None, ALU.mult).then_inc(tap_done, 1)
                    else:
                        dve.wait_ge(tap_done, T0 + (k - 1))
                        dve.scalar_tensor_tensor(acc, src, w, acc, ALU.mult, ALU.add).then_inc(tap_done, 1)

            def conv_end(l, c):
                dve.wait_ge(tap_done, (l * KD + c) * TAPS + TAPS)
                dve.tensor_tensor(gx, acc0, acc1, ALU.add).then_inc(conv_done, 1)

            def gn_center(l, g):
                dve.wait_ge(mean_done, l * KD + g + 1)
                dve.tensor_tensor(gx, gx, bank[6][:], ALU.subtract).then_inc(xc_done, 1)

            def gn_scale(l, g):
                dve.wait_ge(grs_done, l * KD + g + 1)
                dve.tensor_tensor(gy, gx, grs, ALU.mult).then_inc(gy_done, 1)

            def group(l, q, s, post, c, g, cols=lambda i: UW, n=4):
                for i in range(n):
                    split(*adv(q, s, i + AHEAD), cols(i))
                    if i > 0:
                        post(i - 1)
                    if i == 2 and g is not None:
                        gn_center(l, g)
                    if c is not None:
                        if i == 0:
                            dve.wait_ge(conv_done, l * KD + c) if not isinstance(c, int) or c > 0 else None
                        taps(l, c, i)
                post(n - 1)
                if g is not None:
                    gn_scale(l, g)
                if c is not None:
                    if g is not None:
                        dve.wait_ge(gy_done, l * KD + g + 1)
                    conv_end(l, c)

            dve.memset(lns[:, 0, 18:19], EPS).then_inc(eps_ready, 1)
            for k in range(KD):
                dve.wait_ge(xhi_ready, k + 1)
                dve.tensor_tensor(x_lo[:, k], h[:, k], f32(x_hi[:, k]), ALU.subtract).then_inc(xlo_ready, 1)
            for s in range(AHEAD):
                split(0, s)
            dve.wait_ge(par_landed, 16)
            lam = pr[:].rearrange("p (l n) -> p l n", l=L)[:, :, PC["lam"]:PC["lam"] + KR]
            l3 = [lt[:, i].rearrange("p (l n) -> p l n", l=L) for i in range(4)]
            steps = [0]

            def lam_step(ins):
                steps[0] += 1
                ins.then_inc(lam_dve, 1)
                dve.wait_ge(lam_dve, steps[0])

            lam_step(dve.scalar_tensor_tensor(l3[0], lam, -1.0, lam, ALU.mult, ALU.max))
            dve.wait_ge(lam_act, 1)
            lam_step(dve.tensor_scalar(lt[:, 2], lt[:, 1], 2.0, None, ALU.add))
            lam_step(dve.reciprocal(lt[:, 2], lt[:, 2]))
            lam_step(dve.tensor_tensor(lt[:, 1], lt[:, 1], lt[:, 2], ALU.mult))
            lam_step(dve.tensor_tensor(lt[:, 2], lt[:, 1], lt[:, 1], ALU.mult))
            lam_step(dve.tensor_scalar(lt[:, 3], lt[:, 2], 1.0 / 15.0, None, ALU.mult))
            for k in (13, 11, 9, 7, 5, 3):
                lam_step(dve.scalar_tensor_tensor(lt[:, 3], lt[:, 3], 1.0 / k, lt[:, 2], ALU.add, ALU.mult))
            lam_step(dve.scalar_tensor_tensor(lt[:, 3], lt[:, 3], 1.0, lt[:, 1], ALU.add, ALU.mult))
            lam_step(dve.tensor_scalar(l3[0], lam, -1.0, 0.0, ALU.mult, ALU.max))
            lam_step(dve.scalar_tensor_tensor(lt[:, 0], lt[:, 3], 2.0, lt[:, 0], ALU.mult, ALU.add))
            lam_step(dve.tensor_scalar(sp8[:, 0], lt[:, 0], 8.0, None, ALU.mult))
            lam_step(dve.tensor_scalar(sp8[:, 1], lt[:, 0], -8.0, None, ALU.mult))
            dve.wait_ge(res_landed, 16)
            dve.wait_ge(eps_ready, 1)

            with dve.Fori(0, L) as l:
                ffn(l, 0)

                def c_group(it, c, g):
                    q, s = q0(l, U_C)

                    def post(i):
                        if i % 2:
                            j = it * 2 + i // 2
                            dve.wait_ge(csig_done, l * KD + j + 1)
                            dve.scalar_tensor_tensor(
                                cpad[:, bass.ds(j, 1), TAPS - 1:].rearrange("p a n -> p (a n)"),
                                bank[2 * (i // 2)][:], col("b_c", l, j * 2), sgc, ALU.add, ALU.mult
                            ).then_inc(cmul_done, 1)
                    group(l, q + it, s, post, c, g)

                c_group(0, None, None)
                dve.wait_ge(pads_ready, l * 2 + 1)
                dve.wait_ge(cmul_done, l * KD + (C_CMUL + 2))
                c_group(1, 0, None)
                dve.wait_ge(cmul_done, l * KD + (C_CMUL + 4))
                settle(dve)
                with dve.Fori(2, 4) as it:
                    c_group(it, it - 1, it - 2)
                dve.wait_ge(cmul_done, l * KD + (C_CMUL + KD))
                settle(dve)

                no_post = lambda i: None
                q, s = q0(l, U_RG)
                with dve.Fori(0, 2) as it:
                    group(l, q + it, s, no_post, it + 3, it + 2)
                group(l, q + 2, s, no_post, None, 4, lambda i: UW if R_UNITS[i][0] == "rx" else 3 * P, 3)

                def rconv(j):
                    n = l * (KR * 3) + 3 * j
                    dve.wait_ge(rx_done, l * KR + (j + 1 + C_RX))
                    if j >= 4:
                        dve.wait_ge(rclo_ready, l * KR + (j - 3))
                    w = lambda k: col("rw", l, RTAPS * j + k)
                    src = lambda k: rxp[:, j % 2, k:k + S]
                    dst = rcf[j % 4]
                    dve.tensor_scalar(dst, src(0), w(0), col("rb", l, j), ALU.mult, ALU.add).then_inc(rtap_done, 1)
                    for k in range(1, RTAPS):
                        dve.wait_ge(rtap_done, n + k)
                        dve.scalar_tensor_tensor(dst, src(k), w(k), dst, ALU.mult, ALU.add
                                                 ).then_inc(rtap_done if k < RTAPS - 1 else rc_done, 1)

                def rc_lo(j):
                    dve.wait_ge(rchi_ready, l * KR + (j + 1))
                    dve.tensor_tensor(a_lo[:, j % 4], rcf[j % 4], f32(a_hi[:, j % 4]), ALU.subtract
                                      ).then_inc(rclo_ready, 1)

                def r_gate_input(j):
                    r, i, a, v = RT[j % 2]
                    dve.wait_ge(ra_done, l * (KR * 5) + (5 * j + 2 + C_RA * 5))
                    dve.tensor_tensor(i, i, rcf[j % 4], ALU.mult).then_inc(rv_done, 1)
                    dve.wait_ge(ra_done, l * (KR * 5) + (5 * j + 5 + C_RA * 5))
                    dve.scalar_tensor_tensor(v, v, 1.0, r, ALU.add, ALU.mult).then_inc(rv_done, 1)

                def r_scan(j):
                    r, i, a, v = RT[j % 2]
                    n = l * (KR * 2) + 2 * j
                    dve.wait_ge(rs_done, l * KR + (j + 1))
                    dve.scalar_tensor_tensor(v, v, SQ_UP ** -0.5, i, ALU.mult, ALU.mult).then_inc(ru_done, 1)
                    dve.wait_ge(ru_done, n + 1)
                    dve.tensor_tensor_scan(r, a, v, 0.0, ALU.mult, ALU.add).then_inc(ru_done, 1)
                    dve.wait_ge(ru_done, n + 2)
                    dve.wait_ge(gelu_done, l * KR + (j + 1 + C_GELU))
                    dve.tensor_tensor(hgm[:, j], r, gates[:, j], ALU.mult).then_inc(hg_done, 1)

                for i, (kind, j) in enumerate(R_UNITS):
                    n = i + AHEAD
                    ahead = R_UNITS[n][0] if n < len(R_UNITS) else "g"
                    split(*q0(l, U_R + n), 3 * P if ahead.startswith("bd") else UW)
                    if i >= 2 and R_UNITS[i - 2][0] == "rx":
                        rc_lo(R_UNITS[i - 2][1])
                    if i >= 1:
                        pk, pj = R_UNITS[i - 1]
                        if pk == "rx":
                            rconv(pj)
                        elif pk == "bdx":
                            r_gate_input(pj)
                        elif pk == "bda" and pj >= 1:
                            r_scan(pj - 1)
                r_gate_input(KR - 1)
                r_scan(KR - 1)

                q, s = q0(l, U_G)
                group(l, q, s, no_post, 5, None)
                with dve.Fori(1, 3) as it:
                    group(l, q + it, s, no_post, it + 5, it + 4)
                group(l, q + 3, s, no_post, None, 7,
                      lambda i: UW if i == 0 else (Y_SPLIT[i - 1][1] - Y_SPLIT[i - 1][0]) * P)

                for j in range(KD):
                    dve.wait_ge(cs_hi, l * KD + (j + 1))
                    dve.tensor_tensor(x_lo[:, j], cpad[:, j, TAPS - 1:], f32(x_hi[:, j]), ALU.subtract
                                      ).then_inc(cs_lo, 1)
                for j in range(KR):
                    dve.wait_ge(hs_hi, l * KR + (j + 1))
                    src, dst = (hg_hi[:, j], hg_lo[:, j]) if j < 9 else (a_hi[:, j - 9], a_lo[:, j - 9])
                    dve.tensor_tensor(dst, hgm[:, j], f32(src), ALU.subtract).then_inc(hs_lo, 1)

                def mix(f):
                    dve.wait_ge(unit_done, l * UPL + (U_Y + 3 * f + 3 + RING))
                    dve.wait_ge(gate_done, l * (2 * KD) + (2 * f + 2 + C_GATE))
                    for i in range(2):
                        g = gates[:, 2 * f + i]
                        dve.tensor_tensor(g, bank[2 * (f % 2) + i][:], g, ALU.mult).then_inc(mm_done, 1)
                    dve.wait_ge(mm_done, l * (2 * KD) + (2 * f + 2))
                    dve.tensor_tensor(hgm[:, f], gates[:, 2 * f], gates[:, 2 * f + 1], ALU.add).then_inc(m_done, 1)

                N0 = l * (2 * KF + KD) + KF
                for i in range(3 * KD):
                    n = i + AHEAD
                    k0, k1 = Y_SPLIT[n % 3]
                    if n < 3 * KD:
                        split(*q0(l, U_Y + n), (k1 - k0) * P)
                    else:
                        split(*q0(l, U_Y + n))
                        if n < 3 * KD + 2:
                            asplit(q0(l, U_Y + n)[1], hgm, n - 3 * KD, N0 + (n - 3 * KD))
                    if i % 3 == 0 and i > 0:
                        mix(i // 3 - 1)
                mix(KD - 1)

                asplit(q0(l, U_O + 2)[1], hgm, 2, N0 + 2)
                for k in range(KD - AHEAD):
                    split(*q0(l, U_O + k + AHEAD))
                    asplit(q0(l, U_O + k + AHEAD)[1], hgm, k + AHEAD, N0 + (k + AHEAD))
                tail(l, 1, *q0(l, U_O + KD))

                ffn(l, 1)

        @block.tensor
        def _(pe):
            pe.sem_inc(unit_done, RING)

            def products(dst, tiles, first, last):
                for i, (sh, sl, mh, ml) in enumerate(tiles):
                    f, z = first and i == 0, last and i == len(tiles) - 1
                    pe.matmul(dst, sh, mh, start=f, stop=False)
                    pe.matmul(dst, sh, ml, start=False, stop=False)
                    ins = pe.matmul(dst, sl, mh, start=False, stop=z)
                return ins

            def wtile(s, i):
                return w_hi[:, s, i * P:(i + 1) * P], w_lo[:, s, i * P:(i + 1) * P]

            def in_unit(q, s, dst):
                pe.wait_ge(lo_ready, U(q, s) + (RING + 1))
                products(dst, [(*wtile(s, k), x_hi[:, k], x_lo[:, k]) for k in range(KD)], True, True
                         ).then_inc(unit_done, 1)

            def out_unit(q, s, n, b, first, last):
                for i in range(2):
                    ins = products(bank[2 * b + i][:], [(a_hi[:, s, b * P:(b + 1) * P], a_lo[:, s, b * P:(b + 1) * P],
                                                         w_hi[:, s, i * S:i * S + S], w_lo[:, s, i * S:i * S + S])],
                                   first, last)
                return ins

            def xpose(l, n, b):
                pe.wait_ge(y_ready, l * 12 + (4 * n + b + 1 + C_Y))
                for i in range(2):
                    for k in range(4):
                        ins = pe.transpose(bank[2 * b + i][:, k * P:(k + 1) * P],
                                           res[:, b, (4 * i + k) * P:(4 * i + k + 1) * P], ident[:])
                    ins.then_inc(xpose_done, 1)

            def projection(l, n, rel, N0, K, banks01_free):
                q, s = q0(l, rel)

                def ready(k, q, s):
                    pe.wait_ge(lo_ready, U(q, s) + (RING + 1))
                    pe.wait_ge(alo_ready, N0 + k + 1)

                def whole(k, q, s, first=False):
                    ready(k, q, s)
                    for b in (2, 3, 0, 1):
                        if first and b == 0:
                            banks01_free()
                        ins = out_unit(q, s, N0, b, first, False)
                    ins.then_inc(unit_done, 1)

                whole(0, q, s, True)
                lead = (K - 4) % 4 or 4
                for k in range(1, lead):
                    whole(k, *adv(q, s, k))
                if K - 4 - lead:
                    with pe.Fori(0, (K - 4 - lead) // 4) as it:
                        for i in range(4):
                            whole(it * 4 + (lead + i), *adv(q + it, s, lead + i))
                for b in range(NB):
                    for k in range(K - 4, K):
                        qq, ss = adv(q, s, k)
                        if b == 0:
                            ready(k, qq, ss)
                        ins = out_unit(qq, ss, N0, b, False, k == K - 1)
                        if b == NB - 1:
                            ins.then_inc(unit_done, 1)
                    if b < NB - 1:
                        ins.then_inc(blk_done, 1)
                    if b == 2:
                        xpose(l, n, 0)
                for b in range(1, NB):
                    xpose(l, n, b)

            def x_ready(l, n):
                pe.wait_ge(xlo_ready, l * 24 + (8 * n + KD))

            def ffn(l, f):
                q, s = q0(l, U_FFN[f])
                x_ready(l, 2 * f)
                settle(pe)
                with pe.Fori(0, KF // 2) as it:
                    for t in range(2):
                        pe.wait_ge(hmul_done, l * (2 * KF) + (it * 2 + (f * KF + t + 1)))
                        in_unit(*adv(q + it, s, 2 * t), bank[2 * t][:])
                        in_unit(*adv(q + it, s, 2 * t + 1), bank[2 * t + 1][:])
                projection(l, 2 * f, U_FFN[f] + 2 * KF, l * (2 * KF + KD) + f * (KF + KD), KF,
                           lambda: pe.wait_ge(hmul_done, l * (2 * KF) + (f * KF + KF + C_HMUL)))

            def gn_mean(l, g):
                pe.wait_ge(conv_done, l * KD + g + 1)
                pe.matmul(bank[6][:], avg[:], gx, start=True, stop=True).then_inc(mean_done, 1)

            def gn_var(l, g):
                pe.wait_ge(sq_done, l * KD + g + 1)
                pe.matmul(bank[7][:], avg[:], gsq, start=True, stop=True).then_inc(var_done, 1)

            pe.wait_ge(consts, 4)
            with pe.Fori(0, L) as l:
                ffn(l, 0)

                def c_group(it, g):
                    q, s = q0(l, U_C)
                    for i in range(4):
                        if i % 2 == 0:
                            pe.wait_ge(cmul_done, l * KD + it * 2 + (i // 2 + 1))
                        in_unit(*adv(q + it, s, i), bank[i][:])
                        if g is not None and i == 0:
                            gn_mean(l, g)
                        if g is not None and i == 2:
                            gn_var(l, g)

                x_ready(l, 1)
                c_group(0, None)
                c_group(1, None)
                with pe.Fori(2, 4) as it:
                    c_group(it, it - 2)

                pe.wait_ge(cmul_done, l * KD + (KD + C_CMUL))
                settle(pe)

                def rg_group(it, g, n=4):
                    q, s = q0(l, U_RG)
                    for i in range(n):
                        pe.wait_ge(gelu_done, l * KR + it * 4 + (i + 1))
                        in_unit(*adv(q + it, s, i), bank[i][:])
                        if i == 0:
                            gn_mean(l, g)
                        if i == 2:
                            gn_var(l, g)

                with pe.Fori(0, 2) as it:
                    rg_group(it, it + 2)
                rg_group(2, 4, 3)

                pe.wait_ge(gelu_done, l * KR + (KR + C_GELU))
                for i, (kind, j) in enumerate(R_UNITS):
                    q, s = q0(l, U_R + i)
                    if kind == "rx":
                        pe.wait_ge(rx_done, l * KR + (j + 1))
                        in_unit(q, s, bank[4 + j % 2][:])
                        continue
                    if kind == "bda":
                        pe.wait_ge(ra_done, l * (KR * 5) + (5 * j + 2))
                        pe.wait_ge(rclo_ready, l * KR + min(j + 2, KR))
                    pe.wait_ge(lo_ready, U(q, s) + (RING + 1))
                    near = [t for t in (j - 1, j, j + 1) if 0 <= t < KR]
                    products(bank[(0 if kind == "bda" else 2) + j % 2][:],
                             [(*wtile(s, t - j + 1), a_hi[:, t % 4], a_lo[:, t % 4]) for t in near], True, True
                             ).then_inc(unit_done, 1)

                pe.wait_ge(ra_done, l * (KR * 5) + (5 * KR + C_RA * 5))

                def g_group(it, g):
                    q, s = q0(l, U_G)
                    for i in range(4):
                        pe.wait_ge(gate_done, l * (2 * KD) + it * 4 + (i + 1))
                        in_unit(*adv(q + it, s, i), bank[i][:])
                        if g is not None and i == 0:
                            gn_mean(l, g)
                        if g is not None and i == 2:
                            gn_var(l, g)

                g_group(0, None)
                with pe.Fori(1, 3) as it:
                    g_group(it, it + 4)
                g_group(3, 7)

                pe.wait_ge(gate_done, l * (2 * KD) + (2 * KD + C_GATE))
                moving = [(x_hi[:, j], x_lo[:, j]) for j in range(KD)]
                moving += [(hg_hi[:, j], hg_lo[:, j]) if j < 9 else (a_hi[:, j - 9], a_lo[:, j - 9]) for j in range(KR)]
                q, s = q0(l, U_Y)

                def y_tile(yi, ff, first=False):
                    pe.wait_ge(m_done, l * KD + yi * 4 + (ff + 1))
                    for i, (k0, k1) in enumerate(Y_SPLIT):
                        qq, ss = adv(q + yi * 3, s, 3 * ff + i)
                        pe.wait_ge(lo_ready, U(qq, ss) + (RING + 1))
                        for k in range(k0, k1):
                            if first:
                                if k < KD:
                                    pe.wait_ge(cs_lo, l * KD + (k + 1))
                                else:
                                    pe.wait_ge(hs_lo, l * KR + (k - KD + 1))
                            ins = products(bank[2 * (ff % 2) + (0 if k < KD else 1)][:],
                                           [(*wtile(ss, k - k0), *moving[k])],
                                           k in (0, KD), k in (KD - 1, KD + KR - 1))
                        ins.then_inc(unit_done, 1)

                for ff in range(4):
                    y_tile(0, ff, ff == 0)
                for ff in range(4):
                    y_tile(1, ff)

                projection(l, 1, U_O, l * (2 * KF + KD) + KF, KD,
                           lambda: pe.wait_ge(m_done, l * KD + (KD + C_M)))

                ffn(l, 1)


def _units(np, i):
    W = np.zeros((L, UPL, P, UW), np.float32)

    def tiles(w, cols):
        K = w.shape[0] // P
        return [w[:, c:c + P].reshape(K, P, P).transpose(1, 0, 2).reshape(P, K * P) for c in cols]

    for l in range(L):
        for f, n in enumerate(("ffn1", "ffn2")):
            gu, down = i[f"{n}_w_gu"][l], i[f"{n}_w_down"][l]
            b = U_FFN[f]
            for t in range(KF):
                W[l, b + 2 * t], W[l, b + 2 * t + 1] = tiles(gu, (t * P, DFF + t * P))
            W[l, b + 2 * KF:b + 3 * KF] = down.reshape(KF, P, D)
        w = i["mix_w_in"][l]
        oc, og = 0, D
        orx, org = 2 * D, 2 * D + DRNN
        ogc, ogr = 2 * D + 2 * DRNN, 3 * D + 2 * DRNN
        for j in range(KD):
            W[l, U_C + 2 * j], W[l, U_C + 2 * j + 1] = tiles(w, (oc + j * P, og + j * P))
            W[l, U_G + 2 * j], W[l, U_G + 2 * j + 1] = tiles(w, (ogc + j * P, ogr + j * P))
        for j in range(KR):
            W[l, U_RG + j] = tiles(w, (org + j * P,))[0]
        band = {}
        for kind, name in (("bda", "rnn_w_a"), ("bdx", "rnn_w_x")):
            m = np.zeros((DRNN, DRNN), np.float32)
            for b in range(DRNN // RB):
                m[b * RB:(b + 1) * RB, b * RB:(b + 1) * RB] = i[name][l, b]
            band[kind] = m
        for n, (kind, j) in enumerate(R_UNITS):
            if kind == "rx":
                W[l, U_R + n] = tiles(w, (orx + j * P,))[0]
                continue
            for t in (j - 1, j, j + 1):
                if 0 <= t < KR:
                    W[l, U_R + n, :, (t - j + 1) * P:(t - j + 2) * P] = \
                        band[kind][t * P:(t + 1) * P, j * P:(j + 1) * P]
        y = np.concatenate([i["conv_w_proj"][l], i["rnn_w_proj"][l]], 0)
        for f in range(KD):
            t = tiles(y, (f * P,))[0]
            for n, (k0, k1) in enumerate(Y_SPLIT):
                W[l, U_Y + 3 * f + n, :, 0:(k1 - k0) * P] = t[:, k0 * P:k1 * P]
        W[l, U_O:U_O + KD] = i["mix_w_out"][l].reshape(KD, P, D)
    return W.reshape(L * UPL, P, UW)


def _params(np, i):
    A = np.zeros((P, L, NPAR), np.float32)

    def put(name, l, v, at=0, step=1):
        v = v.reshape(v.shape[0] // P, P, -1).transpose(1, 0, 2)
        n = v.shape[1] * v.shape[2]
        A[:, l, PC[name] + at:PC[name] + at + step * (n - 1) + 1:step] = v.reshape(P, n)

    for l in range(L):
        b = i["mix_b_in"][l]
        put("b_c", l, b[0:D], 0, 2)
        put("b_c", l, b[D:2 * D], 1, 2)
        o = 2 * D
        put("b_rx", l, b[o:o + DRNN])
        put("b_rg", l, b[o + DRNN:o + 2 * DRNN])
        o += 2 * DRNN
        put("b_g", l, b[o:o + D], 0, 2)
        put("b_g", l, b[o + D:o + 2 * D], 1, 2)
        put("cw", l, i["conv_dw_w"][l].T)
        put("cb", l, i["conv_dw_b"][l])
        put("gg", l, i["conv_gn_g"][l])
        put("gb", l, i["conv_gn_b"][l])
        put("rw", l, i["rnn_conv_w"][l].T)
        put("rb", l, i["rnn_conv_b"][l])
        put("ba", l, i["rnn_b_a"][l])
        put("bx", l, i["rnn_b_x"][l])
        put("lam", l, i["rnn_lambda"][l])
    return A.reshape(P, L * NPAR)


def kernel(**inputs):
    import numpy as np
    import concourse.bacc as bacc
    from concourse.bass_utils import run_bass_kernel_spmd

    i = {k: np.asarray(v) for k, v in inputs.items()}
    x = i["x"].reshape(S, D)
    lnp = np.empty((L * 3, P, 2, D), np.float32)
    for l in range(L):
        for n in range(3):
            lnp[3 * l + n, :, 0], lnp[3 * l + n, :, 1] = i[f"ln{n + 1}_g"][l], i[f"ln{n + 1}_b"][l]
    arrays = {
        "wst": _units(np, i),
        "xT": np.ascontiguousarray(x.T.reshape(KD, P, S).transpose(1, 0, 2)),
        "xtok": np.ascontiguousarray(x),
        "par": _params(np, i),
        "lnp": lnp,
    }
    nc = bacc.Bacc("TRN2", target_bir_lowering=False, num_devices=1)
    args = [nc.dram_tensor(n, a.shape, F32, kind="ExternalInput").ap() for n, a in arrays.items()]
    out = nc.dram_tensor("out", (S, D), F32, kind="ExternalOutput").ap()
    trunk(nc, *args, out)
    r = run_bass_kernel_spmd(nc, [arrays], core_ids=[0])
    return r.results[0]["out"].reshape(1, S, D)
```

```python
import math

import concourse.bass as bass
from concourse import mybir

F32 = mybir.dt.float32
F32R = mybir.dt.float32r
ALU = mybir.AluOpType
ACT = mybir.ActivationFunctionType

P = 128
RING = 4
AHEAD = 3
EPS = 1e-5

L, S, D = 2, 512, 1024
DFF, DRNN = 2816, 1408
TAPS, RTAPS = 31, 4
KD, KF, KR = D // P, DFF // P, DRNN // P
NB = S // P
RB = DRNN // 16
ALPHA = (2 * L) ** 0.25
UW = 1024

FFN_UNITS = 2 * KF + KF
U_FFN = (0, 0)
MIX = FFN_UNITS
U_C, U_RG = MIX, MIX + 2 * KD
U_R = U_RG + KR
U_G = U_R + 3 * KR
U_YR = U_G + 2 * KD
U_YC = U_YR + 2 * KD
U_O = U_YC + KD
U_FFN = (0, U_O + KD)
UPL = U_FFN[1] + FFN_UNITS
assert UPL % RING == 0
PART = (slice(0, 3 * P), slice(3 * P, 4 * P))

R_GROUPS = [[("rx", 0), ("rx", 1)]]
for _p in range(0, KR, 2):
    R_GROUPS.append([("rx", _j) for _j in (_p + 2, _p + 3) if _j < KR]
                    + [(_k, _j) for _j in (_p, _p + 1) if _j < KR for _k in ("bda", "bdx")])
R_UNITS = [u for g in R_GROUPS for u in g]
assert len(R_UNITS) == 3 * KR
YR_ORDER = [8, 9, 10, 0, 1, 2, 3, 4, 5, 6, 7]
YR_SPLIT = [(0, 6), (6, KR)]
HG_SLOT = {8: 0, 9: 2, 10: 3}
C_SLOT = 1

TAPS_C = [0, 0, 0] + [5 * (i + 1) for i in range(2 * KD - 3)]
TAPS_RG = [65 + (4 * TAPS - 65) * (i + 1) // KR for i in range(KR)]
TAPS_G = [4 * TAPS + 88 * (i + 1) // (2 * KD) for i in range(2 * KD)]
TAPS_YR = [min(4 * TAPS + 88 + 36 * (i + 1) // 11, KD * TAPS) for i in range(2 * KD)]

PC = {}
_n = 0
for _name, _w in (("b_c", 2 * KD), ("b_rg", KR), ("b_rx", KR), ("b_g", 2 * KD), ("cw", KD * TAPS), ("cb", KD),
                  ("gg", KD), ("gb", KD), ("rw", KR * RTAPS), ("rb", KR), ("ba", KR), ("bx", KR), ("lam", KR)):
    PC[_name] = _n
    _n += _w
NPAR = _n
SQ_UP = 2.0 ** 60


def adv(q, s, d):
    return q + (s + d) // RING, (s + d) % RING


def trunk(nc, wst, xT, xtok, par, lnp, out):
    sb, at = nc.alloc_sbuf_tensor, nc.alloc_sbuf_tensor_at
    w_raw = sb("w_raw", [P, RING, UW], F32)
    w_hi = sb("w_hi", [P, RING, UW], F32R)
    w_lo = sb("w_lo", [P, RING, UW], F32R)
    x_hi = sb("x_hi", [P, KD, S], F32R)
    x_lo = sb("x_lo", [P, KD, S], F32R)
    res = sb("res", [P, NB, D], F32)
    a_hi = sb("a_hi", [P, RING, S], F32R)
    a_lo = sb("a_lo", [P, RING, S], F32R)
    pr = sb("pr", [P, L * NPAR], F32)
    sp8 = sb("sp8", [P, 2, L * KR], F32)
    lt = sb("lt", [P, 4, L * KR], F32)
    ident = sb("ident", [P, P], F32)
    avg = sb("avg", [P, P], F32)
    lns = sb("lns", [P, 2, 8], F32)
    epsb = sb("epsb", [P, 1], F32)
    mhalf = sb("mhalf", [P, 1], F32)

    arena = sb("arena", [P, 23040], F32)
    A0 = nc.sbuf_base - 23040 * 4
    gates = at("gates", [P, 2 * KD, S], F32, offset=A0)
    hgm = at("hgm", [P, KR, S], F32, offset=A0 + 32768)
    cpad = at("cpad", [P, KD, TAPS - 1 + S], F32, offset=A0 + 55296)
    ct = at("ct", [P, 6, S], F32, offset=A0 + 72640)
    rxp = at("rxp", [P, 2, RTAPS - 1 + S], F32, offset=A0 + 84928)
    tx = at("tx", [P, 1, S], F32, offset=A0 + 89056)
    h = at("h", [P, KF, S], F32, offset=A0)
    sg = at("sg", [P, 1, S], F32, offset=A0 + 45056)
    yb = at("yb", [P, 2, D], F32, offset=A0 + 47104)
    gb = at("gb", [P, 2, D], F32, offset=A0 + 55296)
    sq = at("sq", [P, D], F32, offset=A0 + 63488)
    yg = at("yg", [P, D], F32, offset=A0 + 67584)

    acc0, acc1, gsq, grs = (ct[:, i] for i in range(4))
    sgc = tx[:, 0]
    rcf = [gates[:, 11 + i] for i in range(4)]
    RT = [[gates[:, 15], tx[:, 0], ct[:, 0], ct[:, 1]], [ct[:, 2], ct[:, 3], ct[:, 4], ct[:, 5]]]

    bank = [nc.alloc_psum_tensor(f"bank{i}", [P, S], F32) for i in range(8)]

    sem = nc.alloc_semaphore
    raw_landed = [sem(f"raw_landed{i}") for i in range(RING)]
    x_landed, res_landed, par_landed, gb_landed = sem("x_landed"), sem("res_landed"), sem("par_landed"), sem("gb_landed")
    out_written = sem("out_written")
    consts, eps_ready = sem("consts"), sem("eps_ready")
    settled = sem("settled")
    hi_ready, lo_ready, unit_done = sem("hi_ready"), sem("lo_ready"), sem("unit_done")
    lam_act, lam_dve = sem("lam_act"), sem("lam_dve")
    silu_done, hmul_done = sem("silu_done"), sem("hmul_done")
    ahi_ready, alo_ready = sem("ahi_ready"), sem("alo_ready")
    blk_done, ln_chain, rstd_ready, y_ready = sem("blk_done"), sem("ln_chain"), sem("rstd_ready"), sem("y_ready")
    lnsq_done, lnvar_done = sem("lnsq_done"), sem("lnvar_done")
    xpose_done, xhi_ready, xlo_ready = sem("xpose_done"), sem("xhi_ready"), sem("xlo_ready")
    pads_ready = sem("pads_ready")
    csig_done, cmul_done = sem("csig_done"), sem("cmul_done")
    tap_done, conv_done = sem("tap_done"), sem("conv_done")
    mean_done, xc_done, sq_done, var_done = sem("mean_done"), sem("xc_done"), sem("sq_done"), sem("var_done")
    gln_done, grs_done, gy_done, gn_done = sem("gln_done"), sem("grs_done"), sem("gy_done"), sem("gn_done")
    gelu_done, rx_done, rtap_done, rc_done = sem("gelu_done"), sem("rx_done"), sem("rtap_done"), sem("rc_done")
    rchi_ready, rclo_ready = sem("rchi_ready"), sem("rclo_ready")
    ra_done, rs_done, rv_done, ru_done, hg_done = (sem(x) for x in ("ra_done", "rs_done", "rv_done", "ru_done", "hg_done"))
    gate_done = sem("gate_done")
    cs_hi, cs_lo, hs_hi, hs_lo = (sem(x) for x in ("cs_hi", "cs_lo", "hs_hi", "hs_lo"))
    mr_done, mc_done, m_done = sem("mr_done"), sem("mc_done"), sem("m_done")

    C_HMUL, C_CMUL, C_GELU, C_RX, C_RA, C_GATE, C_M, C_MR, C_Y = 2, 2, 4, 2, 2, 4, 2, 2, NB

    def U(q, s):
        return q * RING + s

    def q0(l, rel):
        return l * (UPL // RING) + rel // RING, rel % RING

    def one(t, i):
        return t[:, bass.ds(i, 1)].rearrange("p a n -> p (a n)")

    def col(name, l, i):
        return pr[:, bass.ds(l * NPAR + (i + PC[name]), 1)]

    def conv_out(g):
        return cpad[:, bass.ds(g, 1), TAPS - 1:].rearrange("p a n -> p (a n)")

    def hg_pair(j):
        return (x_hi[:, j], x_lo[:, j]) if j < KD else (a_hi[:, HG_SLOT[j]], a_lo[:, HG_SLOT[j]])

    def c_pair(j):
        return (x_hi[:, j], x_lo[:, j]) if j else (a_hi[:, C_SLOT], a_lo[:, C_SLOT])

    def unit_cols(rel):
        if U_R <= rel < U_G:
            return UW if R_UNITS[rel - U_R][0] == "rx" else 3 * P
        if U_YR <= rel < U_YC:
            k0, k1 = YR_SPLIT[(rel - U_YR) % 2]
            return (k1 - k0) * P
        return UW

    def r_done(l, kind, j):
        return l * UPL + (U_R + R_UNITS.index((kind, j)) + RING + 1)

    def done(l, rel):
        return l * UPL + (rel + RING + 1)

    G_BANK = (4, 5, 0, 1)

    def f32(ap):
        return ap.bitcast(F32)

    def settle(eng):
        eng.sem_inc(settled, 1)

    with nc.Block() as block:

        @block.sync
        def _(sp):
            def load(q, s, cols=UW):
                sp.wait_ge(lo_ready, U(q, s) + 1)
                sp.dma_start(w_raw[:, s, 0:cols],
                             wst[bass.ds(U(q, s), 1), :, 0:cols].rearrange("u p n -> (u p) n")
                             ).then_inc(raw_landed[s], 16)

            def loads(q, s, n):
                with sp.Fori(0, n // RING) as it:
                    for i in range(RING):
                        load(*adv(q + it, s, i))
                for i in range(n // RING * RING, n):
                    load(*adv(q, s, i))

            sp.dma_start(h[:, 0:KD // 2], xT[:, 0:KD // 2]).then_inc(x_landed, 16)
            sp.dma_start(h[:, KD // 2:KD], xT[:, KD // 2:KD]).then_inc(x_landed, 16)
            with sp.Fori(0, L) as l:
                loads(*q0(l, 0), U_R)
                for i, (kind, _) in enumerate(R_UNITS):
                    load(*q0(l, U_R + i), UW if kind == "rx" else 3 * P)
                loads(*q0(l, U_G), 2 * KD)
                with sp.Fori(0, KD // 2) as it:
                    qy, sy = q0(l, U_YR)
                    for i in range(4):
                        load(*adv(qy + it, sy, i), unit_cols(U_YR + i))
                loads(*q0(l, U_YC), UPL - U_YC)
            for s in range(AHEAD):
                sp.wait_ge(lo_ready, L * UPL + s + 1)
                sp.dma_start(w_raw[:, s], wst[s]).then_inc(raw_landed[s], 16)

        @block.gpsimd
        def _(pool):
            pool.sem_inc(y_ready, C_Y)
            pool.dma_start(pr[:], par).then_inc(par_landed, 16)
            pool.dma_start(res[:], xtok.rearrange("(b p) d -> p b d", p=P)).then_inc(res_landed, 16)
            pool.memset(ident[:], 0.0).then_inc(consts, 1)
            pool.memset(avg[:], 1.0 / P).then_inc(consts, 1)
            pool.memset(mhalf[:], -0.5).then_inc(consts, 1)
            pool.wait_ge(consts, 3)
            pool.affine_select(out=ident[:], in_=ident[:], compare_op=ALU.not_equal, fill=1.0, base=0,
                               pattern=[[-1, P]], channel_multiplier=1).then_inc(consts, 1)
            pool.wait_ge(consts, 4)

            def layer_norm(l, n, ready):
                ready()
                pool.dma_start(gb[:], lnp[bass.ds(l * 3 + n, 1)].rearrange("a p c d -> p (a c) d")
                               ).then_inc(gb_landed, 16)
                for b in range(NB):
                    X, st = l * 12 + (4 * n + b), lns[:, b % 2]
                    if b >= 2:
                        pool.wait_ge(y_ready, X + (C_Y - 1))
                    pool.wait_ge(lnsq_done, X + 1)
                    settle(pool)
                    pool.tensor_scalar(st[:, 4:5], st[:, 3:4], 1.0 / D, EPS / ALPHA ** 2, ALU.mult, ALU.add
                                       ).then_inc(lnvar_done, 1)
                    pool.wait_ge(lnvar_done, X + 1)
                    pool.tensor_tensor(st[:, 5:6], st[:, 4:5], mhalf[:], ALU.pow).then_inc(rstd_ready, 1)

            with pool.Fori(0, L) as l:
                layer_norm(l, 0, lambda: pool.wait_ge(y_ready, l * 12 + C_Y))
                layer_norm(l, 1, lambda: pool.wait_ge(cs_lo, l * KD + KD))
                layer_norm(l, 2, lambda: pool.wait_ge(y_ready, l * 12 + (C_Y + 8)))
            out_v = out.rearrange("(b p) d -> b p d", p=P)
            for b in range(NB):
                pool.wait_ge(y_ready, C_Y + (L * 3 - 1) * NB + b + 1)
                pool.dma_start(out_v[b], res[:, b]).then_inc(out_written, 16)
            pool.wait_ge(out_written, 16 * NB)

        @block.scalar
        def _(act):
            act.sem_inc(gelu_done, C_GELU)
            act.sem_inc(rx_done, C_RX)
            act.sem_inc(ra_done, C_RA * 5)
            act.sem_inc(gate_done, C_GATE)

            def split(q, s, cols=UW):
                act.wait_ge(raw_landed[s], q * 16 + 16)
                act.wait_ge(unit_done, U(q, s) + 1)
                act.activation(w_hi[:, s, 0:cols], w_raw[:, s, 0:cols], ACT.Copy).then_inc(hi_ready, 1)

            def asplit(q, s, src, k, n):
                act.wait_ge(unit_done, U(q, s) + 1)
                act.activation(a_hi[:, s], one(src, k), ACT.Copy).then_inc(ahi_ready, 1)

            def xt(l, n, b):
                for i in range(2):
                    act.wait_ge(xpose_done, l * 24 + (8 * n + 2 * b + i + 1))
                    act.activation(x_hi[:, 4 * i:4 * i + 4, b * P:(b + 1) * P],
                                   bank[2 * b + i][:].rearrange("p (k n) -> p k n", k=4), ACT.Copy
                                   ).then_inc(xhi_ready, 1)

            def ln_square(l, n, b):
                X, st = l * 12 + (4 * n + b), lns[:, b % 2]
                act.wait_ge(ln_chain, X * 4 + 3)
                if b:
                    act.wait_ge(lnsq_done, X)
                act.activation(sq[:], yb[:, b % 2], ACT.Square, bias=st[:, 2:3], accum_out=st[:, 3:4]
                               ).then_inc(lnsq_done, 1)

            def tail(l, n, q, s):
                ln_square(l, n, 0)
                ln_square(l, n, 1)
                xt(l, n, 0)
                ln_square(l, n, 2)
                xt(l, n, 1)
                split(*adv(q, s, 0))
                xt(l, n, 2)
                ln_square(l, n, 3)
                split(*adv(q, s, 1))
                xt(l, n, 3)
                split(*adv(q, s, 2))

            def ffn(l, f):
                q, s = q0(l, U_FFN[f])

                def pair(q, s, t, down):
                    T = l * (2 * KF) + (f * KF + t)
                    for i in range(2):
                        split(*adv(q, s, AHEAD + i))
                        if down[i] is not None:
                            asplit(*adv(q, s, AHEAD + i), h, down[i], None)
                    act.wait_ge(unit_done, U(q, s) + (RING + 1))
                    act.wait_ge(hmul_done, T + C_HMUL)
                    act.activation(sg[:, 0], bank[down[2]][:], ACT.Silu).then_inc(silu_done, 1)

                with act.Fori(0, KF // 2 - 1) as it:
                    pair(*adv(q + it, s, 0), it * 2, (None, None, 0))
                    pair(*adv(q + it, s, 2), it * 2 + 1, (None, None, 2))
                pair(*adv(q, s, 2 * KF - 4), KF - 2, (None, 0, 0))
                pair(*adv(q, s, 2 * KF - 2), KF - 1, (1, 2, 2))
                qd, sd = adv(q, s, 2 * KF)
                for k in (0, 1):
                    split(*adv(qd, sd, k + AHEAD))
                    asplit(*adv(qd, sd, k + AHEAD), h, k + AHEAD, None)
                with act.Fori(0, 4) as it:
                    for i in range(4):
                        split(*adv(qd + it, sd, 2 + i + AHEAD))
                        asplit(*adv(qd + it, sd, 2 + i + AHEAD), h, it * 4 + (2 + i + AHEAD), None)
                split(*adv(qd, sd, 18 + AHEAD))
                asplit(*adv(qd, sd, 18 + AHEAD), h, 18 + AHEAD, None)
                tail(l, 2 * f, *adv(qd, sd, KF))

            def gn_square(l, g):
                act.wait_ge(xc_done, l * KD + g + 1)
                act.activation(gsq, conv_out(g), ACT.Square).then_inc(sq_done, 1)

            def gn_rstd(l, g):
                act.wait_ge(var_done, l * KD + g + 1)
                act.activation(grs, bank[7][:], ACT.Ln, bias=epsb[:]).then_inc(gln_done, 1)
                act.wait_ge(gln_done, l * KD + g + 1)
                act.activation(grs, grs, ACT.Exp, scale=-0.5).then_inc(grs_done, 1)

            def gn_silu(l, g):
                act.wait_ge(gy_done, l * KD + g + 1)
                act.activation(conv_out(g), conv_out(g), ACT.Silu, bias=col("gb", l, g), scale=col("gg", l, g)
                               ).then_inc(gn_done, 1)

            def hg_hi(l, j, n):
                act.activation(hg_pair(j)[0], hgm[:, j], ACT.Copy).then_inc(hs_hi, 1)

            def c_hi(l, j):
                act.wait_ge(gn_done, l * KD + j + 1)
                act.activation(c_pair(j)[0], conv_out(j), ACT.Copy).then_inc(cs_hi, 1)

            act.wait_ge(eps_ready, 1)
            act.wait_ge(x_landed, 32)
            for k in range(KD):
                act.activation(x_hi[:, k], h[:, k], ACT.Copy).then_inc(xhi_ready, 1)
            for s in range(AHEAD):
                act.wait_ge(raw_landed[s], 16)
                act.activation(w_hi[:, s], w_raw[:, s], ACT.Copy).then_inc(hi_ready, 1)
            act.wait_ge(lam_dve, 1)
            act.activation(lt[:, 1], lt[:, 0], ACT.Exp, scale=-1.0).then_inc(lam_act, 1)

            with act.Fori(0, L) as l:
                ffn(l, 0)

                def ahead(rel):
                    split(*q0(l, rel + AHEAD), unit_cols(rel + AHEAD))

                def c_gate(j):
                    act.wait_ge(unit_done, done(l, U_C + 2 * j + 1))
                    act.wait_ge(cmul_done, l * KD + (j + C_CMUL))
                    act.activation(sgc, bank[2 * (j % 2) + 1][:], ACT.Sigmoid,
                                   bias=col("b_c", l, j * 2 + 1)).then_inc(csig_done, 1)

                for i in range(2 * KD):
                    ahead(U_C + i)
                    if i % 2 == 0 and i:
                        c_gate(i // 2 - 1)

                def rg_gelu(j):
                    act.wait_ge(unit_done, done(l, U_RG + j))
                    act.activation(gates[:, j], bank[j % 4][:], ACT.Gelu_apprx_tanh,
                                   bias=col("b_rg", l, j)).then_inc(gelu_done, 1)

                for i in range(KR):
                    ahead(U_RG + i)
                    if i == 0:
                        c_gate(KD - 1)
                    else:
                        rg_gelu(i - 1)

                def rx_evac(j):
                    act.wait_ge(unit_done, r_done(l, "rx", j))
                    act.wait_ge(pads_ready, l * 2 + 2)
                    if j >= 2:
                        act.wait_ge(rc_done, l * KR + (j - 1))
                    act.activation(rxp[:, j % 2, RTAPS - 1:], bank[4 + j % 2][:], ACT.Identity,
                                   bias=col("b_rx", l, j)).then_inc(rx_done, 1)

                def rc_hi(j):
                    act.wait_ge(rc_done, l * KR + (j + 1))
                    if j >= 4:
                        act.wait_ge(unit_done, r_done(l, "bdx", j - 3))
                    act.activation(a_hi[:, j % 4], rcf[j % 4], ACT.Copy).then_inc(rchi_ready, 1)

                def r_sigmoids(js):
                    for j in js:
                        r, i, a, v = RT[j % 2]
                        act.wait_ge(unit_done, r_done(l, "bdx", j))
                        if j >= 2:
                            act.wait_ge(hg_done, l * KR + (j - 1))
                        act.activation(r, bank[j % 2][:], ACT.Sigmoid, bias=col("ba", l, j)).then_inc(ra_done, 1)
                        act.activation(i, bank[2 + j % 2][:], ACT.Sigmoid, bias=col("bx", l, j)).then_inc(ra_done, 1)

                def r_exps(js):
                    n = l * (KR * 5) + (5 * js[0] + 2 * len(js) + C_RA * 5)
                    act.wait_ge(ra_done, n)
                    for m, j in enumerate(js):
                        r, i, a, v = RT[j % 2]
                        act.activation(a, r, ACT.Exp, scale=sp8[:, 1, bass.ds(l * KR + j, 1)]).then_inc(ra_done, 1)
                        act.wait_ge(ra_done, n + (3 * m + 1))
                        act.activation(v, a, ACT.Square).then_inc(ra_done, 1)
                        act.activation(r, r, ACT.Tanh, scale=sp8[:, 0, bass.ds(l * KR + j, 1)]).then_inc(ra_done, 1)

                def r_sqrts(js):
                    for j in js:
                        v = RT[j % 2][3]
                        act.wait_ge(rv_done, l * (KR * 2) + (2 * (js[-1] + 1) if j == js[0] else 2 * (j + 1)))
                        act.activation(v, v, ACT.Sqrt, scale=SQ_UP).then_inc(rs_done, 1)

                rel = U_R
                for g, units in enumerate(R_GROUPS):
                    new = [j for kind, j in units if kind == "rx"]
                    old = [j for kind, j in (R_GROUPS[g - 1] if g else []) if kind == "bdx"]
                    for i in range(len(units)):
                        ahead(rel + i)
                        if i == 0 and g == 0:
                            rg_gelu(KR - 1)
                        if i == 0 and g == 1:
                            rx_evac(1)
                            rc_hi(0)
                        if i == 0 and old:
                            r_sigmoids(old)
                        if i == 1 and new:
                            rx_evac(new[0])
                        if i == 1 and g == 1:
                            rc_hi(1)
                        if i == 1 and old:
                            r_exps(old)
                        if i == 2 and g > 0:
                            if len(new) > 1:
                                rx_evac(new[1])
                            if new:
                                rc_hi(new[0])
                            if old:
                                r_sqrts(old)
                        if i == 3 and len(new) > 1:
                            rc_hi(new[1])
                    rel += len(units)
                r_sqrts(old)
                last = [KR - 1]
                r_sigmoids(last)
                r_exps(last)
                r_sqrts(last)

                def gate(i):
                    act.wait_ge(unit_done, done(l, U_G + i))
                    act.wait_ge(hg_done, l * KR + min(i + 1, KR))
                    act.activation(gates[:, i], bank[G_BANK[i % 4]][:], ACT.Sigmoid,
                                   bias=col("b_g", l, i)).then_inc(gate_done, 1)

                def norm_steps(i, base):
                    g = base + i // 4
                    if i % 4 == 0 and g:
                        gn_silu(l, g - 1)
                    if i % 4 == 2:
                        gn_square(l, g)
                    if i % 4 == 3:
                        gn_rstd(l, g)

                for i in range(2 * KD):
                    ahead(U_G + i)
                    if i:
                        gate(i - 1)
                    norm_steps(i, 0)
                    if i == 12:
                        for n, j in enumerate(HG_SLOT):
                            hg_hi(l, j, n)

                for i in range(2 * KD):
                    ahead(U_YR + i)
                    if i == 0:
                        act.wait_ge(unit_done, done(l, U_YR - 1))
                        for n in range(KD):
                            hg_hi(l, n, len(HG_SLOT) + n)
                        gate(2 * KD - 1)
                    norm_steps(i, 4)
                    if i == 13:
                        c_hi(l, 0)
                gn_silu(l, KD - 1)

                act.wait_ge(unit_done, done(l, U_YC - 1))
                for j in range(1, KD):
                    c_hi(l, j)
                for i in range(KD):
                    ahead(U_YC + i)
                    if i >= KD - AHEAD:
                        k = i + AHEAD - KD
                        act.wait_ge(m_done, l * KD + (k + 1 + C_M))
                        asplit(*q0(l, U_O + k), hgm, k, None)

                for k in range(AHEAD, KD):
                    split(*q0(l, U_O + k))
                    act.wait_ge(m_done, l * KD + (k + 1 + C_M))
                    asplit(*q0(l, U_O + k), hgm, k, None)
                tail(l, 1, *q0(l, U_O + KD))

                ffn(l, 1)

        @block.vector
        def _(dve):
            dve.sem_inc(lo_ready, RING)
            dve.sem_inc(hmul_done, C_HMUL)
            dve.sem_inc(cmul_done, C_CMUL)
            dve.sem_inc(m_done, C_M)
            dve.sem_inc(mr_done, C_MR)

            def split(q, s, cols=UW):
                dve.wait_ge(hi_ready, U(q, s) + 1)
                dve.tensor_tensor(w_lo[:, s, 0:cols], w_raw[:, s, 0:cols], f32(w_hi[:, s, 0:cols]),
                                  ALU.subtract).then_inc(lo_ready, 1)

            def asplit(s, src, k, n):
                dve.wait_ge(ahi_ready, n + 1)
                dve.tensor_tensor(a_lo[:, s], one(src, k), f32(a_hi[:, s]), ALU.subtract).then_inc(alo_ready, 1)

            def ln(l, n, b):
                X = l * 12 + (4 * n + b)
                y, st = yb[:, b % 2], lns[:, b % 2]
                gain = (1.0 if n == 1 else 0.5) / ALPHA
                if b < NB - 1:
                    dve.wait_ge(blk_done, l * 9 + (3 * n + b + 1))
                else:
                    dve.wait_ge(unit_done, l * UPL + ((MIX, U_FFN[1], UPL)[n] + RING))
                if b >= 2:
                    dve.wait_ge(y_ready, X + (C_Y - 1))
                for i in range(2):
                    cols = slice(S * i, S * i + S)
                    dve.scalar_tensor_tensor(y[:, cols], bank[2 * b + i][:], gain, res[:, b, cols], ALU.mult, ALU.add,
                                             accum_out=st[:, i:i + 1]).then_inc(ln_chain, 1)
                dve.wait_ge(ln_chain, X * 4 + 2)
                dve.tensor_scalar(st[:, 2:3], st[:, 0:1], st[:, 1:2], -1.0 / D, ALU.add, ALU.mult
                                  ).then_inc(ln_chain, 1)
                dve.wait_ge(ln_chain, X * 4 + 3)
                if b == 0:
                    dve.wait_ge(gb_landed, l * 48 + (16 * n + 16))
                else:
                    dve.wait_ge(y_ready, X + C_Y)
                dve.scalar_tensor_tensor(yg[:], y, st[:, 2:3], gb[:, 0], ALU.add, ALU.mult).then_inc(ln_chain, 1)
                dve.wait_ge(ln_chain, X * 4 + 4)
                dve.wait_ge(rstd_ready, X + 1)
                dve.scalar_tensor_tensor(res[:, b], yg[:], st[:, 5:6], gb[:, 1], ALU.mult, ALU.add
                                         ).then_inc(y_ready, 1)
                if b == NB - 1 and n == 0:
                    dve.wait_ge(y_ready, X + (C_Y + 1))
                    dve.memset(cpad[:, :, 0:TAPS - 1], 0.0).then_inc(pads_ready, 1)
                    dve.memset(rxp[:, :, 0:RTAPS - 1], 0.0).then_inc(pads_ready, 1)

            def xt(l, n, b):
                for i in range(2):
                    dve.wait_ge(xhi_ready, l * 24 + (KD + 8 * n + 2 * b + i + 1))
                    at = (slice(None), slice(4 * i, 4 * i + 4), slice(b * P, (b + 1) * P))
                    dve.tensor_tensor(x_lo[at], bank[2 * b + i][:].rearrange("p (k n) -> p k n", k=4),
                                      f32(x_hi[at]), ALU.subtract).then_inc(xlo_ready, 1)

            def tail(l, n, q, s):
                ln(l, n, 0)
                ln(l, n, 1)
                xt(l, n, 0)
                ln(l, n, 2)
                xt(l, n, 1)
                split(*adv(q, s, 0))
                xt(l, n, 2)
                ln(l, n, 3)
                split(*adv(q, s, 1))
                xt(l, n, 3)
                split(*adv(q, s, 2))

            def ffn(l, f):
                q, s = q0(l, U_FFN[f])
                N0 = l * (2 * KF + KD) + f * (KF + KD)

                def pair(q, s, t, down, bk):
                    T = l * (2 * KF) + (f * KF + t)
                    for i in range(2):
                        split(*adv(q, s, AHEAD + i))
                        if down[i] is not None:
                            asplit(adv(q, s, AHEAD + i)[1], h, down[i], N0 + down[i])
                    dve.wait_ge(silu_done, T + 1)
                    dve.wait_ge(unit_done, U(*adv(q, s, 1)) + (RING + 1))
                    dve.tensor_tensor(one(h, t), bank[bk + 1][:], sg[:, 0], ALU.mult).then_inc(hmul_done, 1)

                with dve.Fori(0, KF // 2 - 1) as it:
                    pair(*adv(q + it, s, 0), it * 2, (None, None), 0)
                    pair(*adv(q + it, s, 2), it * 2 + 1, (None, None), 2)
                pair(*adv(q, s, 2 * KF - 4), KF - 2, (None, 0), 0)
                pair(*adv(q, s, 2 * KF - 2), KF - 1, (1, 2), 2)
                qd, sd = adv(q, s, 2 * KF)
                for k in (0, 1):
                    split(*adv(qd, sd, k + AHEAD))
                    asplit(adv(qd, sd, k + AHEAD)[1], h, k + AHEAD, N0 + (k + AHEAD))
                with dve.Fori(0, 4) as it:
                    for i in range(4):
                        split(*adv(qd + it, sd, 2 + i + AHEAD))
                        k = it * 4 + (2 + i + AHEAD)
                        asplit(adv(qd, sd, 2 + i + AHEAD)[1], h, k, N0 + k)
                split(*adv(qd, sd, 18 + AHEAD))
                asplit(adv(qd, sd, 18 + AHEAD)[1], h, 18 + AHEAD, N0 + (18 + AHEAD))
                tail(l, 2 * f, *adv(qd, sd, KF))

            def taps(l, n0, n1):
                for n in range(n0, n1):
                    c, k = divmod(n, TAPS)
                    T = l * (KD * TAPS) + n
                    acc = (acc0, acc1)[k % 2]
                    w = col("cw", l, n)
                    src = cpad[:, c, k:k + S]
                    if k == 0:
                        dve.wait_ge(cmul_done, l * KD + (c + 1 + C_CMUL))
                        if c:
                            dve.wait_ge(conv_done, l * KD + c)
                        else:
                            dve.wait_ge(pads_ready, l * 2 + 1)
                        dve.tensor_scalar(acc, src, w, col("cb", l, c), ALU.mult, ALU.add).then_inc(tap_done, 1)
                    elif k == 1:
                        dve.tensor_scalar(acc, src, w, None, ALU.mult).then_inc(tap_done, 1)
                    else:
                        dve.wait_ge(tap_done, T - 1)
                        dve.scalar_tensor_tensor(acc, src, w, acc, ALU.mult, ALU.add).then_inc(tap_done, 1)
                    if k == TAPS - 1:
                        dve.wait_ge(tap_done, T + 1)
                        dve.tensor_tensor(conv_out(c), acc0, acc1, ALU.add).then_inc(conv_done, 1)

            def gn_center(l, g):
                dve.wait_ge(mean_done, l * KD + g + 1)
                dve.tensor_tensor(conv_out(g), conv_out(g), bank[6][:], ALU.subtract).then_inc(xc_done, 1)

            def gn_scale(l, g):
                dve.wait_ge(grs_done, l * KD + g + 1)
                dve.tensor_tensor(conv_out(g), conv_out(g), grs, ALU.mult).then_inc(gy_done, 1)

            dve.memset(epsb[:], EPS).then_inc(eps_ready, 1)
            for k in range(KD):
                dve.wait_ge(xhi_ready, k + 1)
                dve.tensor_tensor(x_lo[:, k], h[:, k], f32(x_hi[:, k]), ALU.subtract).then_inc(xlo_ready, 1)
            for s in range(AHEAD):
                split(0, s)
            dve.wait_ge(par_landed, 16)
            lam = pr[:].rearrange("p (l n) -> p l n", l=L)[:, :, PC["lam"]:PC["lam"] + KR]
            l3 = [lt[:, i].rearrange("p (l n) -> p l n", l=L) for i in range(4)]
            steps = [0]

            def lam_step(ins):
                steps[0] += 1
                ins.then_inc(lam_dve, 1)
                dve.wait_ge(lam_dve, steps[0])

            lam_step(dve.scalar_tensor_tensor(l3[0], lam, -1.0, lam, ALU.mult, ALU.max))
            dve.wait_ge(lam_act, 1)
            lam_step(dve.tensor_scalar(lt[:, 2], lt[:, 1], 2.0, None, ALU.add))
            lam_step(dve.reciprocal(lt[:, 2], lt[:, 2]))
            lam_step(dve.tensor_tensor(lt[:, 1], lt[:, 1], lt[:, 2], ALU.mult))
            lam_step(dve.tensor_tensor(lt[:, 2], lt[:, 1], lt[:, 1], ALU.mult))
            lam_step(dve.tensor_scalar(lt[:, 3], lt[:, 2], 1.0 / 15.0, None, ALU.mult))
            for k in (13, 11, 9, 7, 5, 3):
                lam_step(dve.scalar_tensor_tensor(lt[:, 3], lt[:, 3], 1.0 / k, lt[:, 2], ALU.add, ALU.mult))
            lam_step(dve.scalar_tensor_tensor(lt[:, 3], lt[:, 3], 1.0, lt[:, 1], ALU.add, ALU.mult))
            lam_step(dve.tensor_scalar(l3[0], lam, -1.0, 0.0, ALU.mult, ALU.max))
            lam_step(dve.scalar_tensor_tensor(lt[:, 0], lt[:, 3], 2.0, lt[:, 0], ALU.mult, ALU.add))
            lam_step(dve.tensor_scalar(sp8[:, 0], lt[:, 0], 8.0, None, ALU.mult))
            lam_step(dve.tensor_scalar(sp8[:, 1], lt[:, 0], -8.0, None, ALU.mult))
            dve.wait_ge(res_landed, 16)
            dve.wait_ge(eps_ready, 1)

            with dve.Fori(0, L) as l:
                ffn(l, 0)

                def ahead(rel):
                    split(*q0(l, rel + AHEAD), unit_cols(rel + AHEAD))

                def c_gated(j):
                    dve.wait_ge(csig_done, l * KD + (j + 1))
                    dve.scalar_tensor_tensor(conv_out(j), bank[2 * (j % 2)][:], col("b_c", l, 2 * j), sgc,
                                             ALU.add, ALU.mult).then_inc(cmul_done, 1)

                n = 0
                for i in range(2 * KD):
                    ahead(U_C + i)
                    if i % 2 == 0 and i:
                        c_gated(i // 2 - 1)
                    taps(l, n, TAPS_C[i])
                    n = TAPS_C[i]

                for i in range(KR):
                    ahead(U_RG + i)
                    if i == 0:
                        c_gated(KD - 1)
                    taps(l, n, TAPS_RG[i])
                    n = TAPS_RG[i]

                def rconv(j):
                    n = l * (KR * 3) + 3 * j
                    dve.wait_ge(rx_done, l * KR + (j + 1 + C_RX))
                    if j >= 4:
                        dve.wait_ge(rclo_ready, l * KR + (j - 3))
                        dve.wait_ge(rv_done, l * (KR * 2) + 2 * ((j - 4) // 2 * 2) + (j - 4) % 2 + 1)
                    w = lambda k: col("rw", l, RTAPS * j + k)
                    src = lambda k: rxp[:, j % 2, k:k + S]
                    dst = rcf[j % 4]
                    dve.tensor_scalar(dst, src(0), w(0), col("rb", l, j), ALU.mult, ALU.add).then_inc(rtap_done, 1)
                    for k in range(1, RTAPS):
                        dve.wait_ge(rtap_done, n + k)
                        dve.scalar_tensor_tensor(dst, src(k), w(k), dst, ALU.mult, ALU.add
                                                 ).then_inc(rtap_done if k < RTAPS - 1 else rc_done, 1)

                def rc_lo(j):
                    dve.wait_ge(rchi_ready, l * KR + (j + 1))
                    dve.tensor_tensor(a_lo[:, j % 4], rcf[j % 4], f32(a_hi[:, j % 4]), ALU.subtract
                                      ).then_inc(rclo_ready, 1)

                def r_inputs(js):
                    for j in js:
                        r, i, a, v = RT[j % 2]
                        dve.wait_ge(ra_done, l * (KR * 5) + (5 * js[0] + 2 * (j - js[0]) + 2 + C_RA * 5))
                        dve.tensor_tensor(i, i, rcf[j % 4], ALU.mult).then_inc(rv_done, 1)

                def r_squares(js):
                    for m, j in enumerate(js):
                        r, i, a, v = RT[j % 2]
                        dve.wait_ge(ra_done, l * (KR * 5) + (5 * js[0] + 2 * len(js) + 3 * (m + 1) + C_RA * 5))
                        dve.scalar_tensor_tensor(v, v, 1.0, r, ALU.add, ALU.mult).then_inc(rv_done, 1)

                def r_scans(js):
                    n = l * (KR * 2) + 2 * js[0]
                    for j in js:
                        r, i, a, v = RT[j % 2]
                        dve.wait_ge(rs_done, l * KR + (j + 1))
                        dve.scalar_tensor_tensor(v, v, SQ_UP ** -0.5, i, ALU.mult, ALU.mult).then_inc(ru_done, 1)
                    for m, j in enumerate(js):
                        r, i, a, v = RT[j % 2]
                        dve.wait_ge(ru_done, n + (m + 1))
                        dve.tensor_tensor_scan(r, a, v, 0.0, ALU.mult, ALU.add).then_inc(ru_done, 1)
                    for m, j in enumerate(js):
                        r = RT[j % 2][0]
                        dve.wait_ge(ru_done, n + (len(js) + m + 1))
                        dve.wait_ge(gelu_done, l * KR + (j + 1 + C_GELU))
                        dve.tensor_tensor(hgm[:, j], r, gates[:, j], ALU.mult).then_inc(hg_done, 1)

                rel = U_R
                for g, units in enumerate(R_GROUPS):
                    new = [j for kind, j in units if kind == "rx"]
                    old = [j for kind, j in (R_GROUPS[g - 1] if g else []) if kind == "bdx"]
                    for i in range(len(units)):
                        ahead(rel + i)
                        if g == 1 and i == 0:
                            rconv(1)
                            rc_lo(0)
                        if i == 0 and old:
                            r_inputs(old)
                        if i == 1 and new:
                            rconv(new[0])
                        if g == 1 and i == 1:
                            rc_lo(1)
                        if i == 1 and old:
                            r_squares(old)
                        if i == 2 and g > 0:
                            if new:
                                rc_lo(new[0])
                            if len(new) > 1:
                                rconv(new[1])
                            if old:
                                r_scans(old)
                        if i == 3 and len(new) > 1:
                            rc_lo(new[1])
                    rel += len(units)
                r_scans(old)
                last = [KR - 1]
                r_inputs(last)
                r_squares(last)
                r_scans(last)

                def hg_lo(j, n):
                    dve.wait_ge(hs_hi, l * KR + (n + 1))
                    dve.tensor_tensor(hg_pair(j)[1], hgm[:, j], f32(hg_pair(j)[0]), ALU.subtract).then_inc(hs_lo, 1)

                def c_lo(j):
                    dve.wait_ge(cs_hi, l * KD + (j + 1))
                    dve.tensor_tensor(c_pair(j)[1], conv_out(j), f32(c_pair(j)[0]), ALU.subtract).then_inc(cs_lo, 1)

                def norm_steps(i, base):
                    g = base + i // 4
                    if i % 4 == 1:
                        gn_center(l, g)
                    if i % 4 == 3:
                        gn_scale(l, g)

                for i in range(2 * KD):
                    ahead(U_G + i)
                    if i % 4 == 1:
                        norm_steps(i, 0)
                    if i == 12:
                        for m, j in enumerate(HG_SLOT):
                            hg_lo(j, m)
                    taps(l, n, TAPS_G[i])
                    n = TAPS_G[i]
                    if i % 4 == 3:
                        norm_steps(i, 0)

                def mix_r(f):
                    dve.wait_ge(unit_done, done(l, U_YR + 2 * f + 1))
                    dve.wait_ge(gate_done, l * (2 * KD) + (2 * f + 2 + C_GATE))
                    g = gates[:, 2 * f + 1]
                    dve.tensor_tensor(g, bank[2 + f % 2][:], g, ALU.mult).then_inc(mr_done, 1)

                for i in range(2 * KD):
                    ahead(U_YR + i)
                    if i == 0:
                        for m in range(KD):
                            hg_lo(m, len(HG_SLOT) + m)
                    if i % 2 == 0 and i:
                        mix_r(i // 2 - 1)
                    if i % 4 == 1:
                        norm_steps(i, 4)
                    taps(l, n, TAPS_YR[i])
                    n = TAPS_YR[i]
                    if i == 13:
                        c_lo(0)
                    if i % 4 == 3:
                        norm_steps(i, 4)
                assert n == KD * TAPS

                def mix(f):
                    dve.wait_ge(unit_done, done(l, U_YC + f))
                    g = gates[:, 2 * f]
                    dve.tensor_tensor(g, bank[f % 2][:], g, ALU.mult).then_inc(mc_done, 1)
                    dve.wait_ge(mc_done, l * KD + (f + 1))
                    dve.wait_ge(mr_done, l * KD + (f + 1 + C_MR))
                    dve.tensor_tensor(hgm[:, f], g, gates[:, 2 * f + 1], ALU.add).then_inc(m_done, 1)

                mix_r(KD - 1)
                for j in range(1, KD):
                    c_lo(j)
                N0 = l * (2 * KF + KD) + KF
                for i in range(KD):
                    ahead(U_YC + i)
                    if i:
                        mix(i - 1)
                    if i >= KD - AHEAD:
                        k = i + AHEAD - KD
                        asplit(q0(l, U_O + k)[1], hgm, k, N0 + k)
                mix(KD - 1)

                for k in range(AHEAD, KD):
                    split(*q0(l, U_O + k))
                    asplit(q0(l, U_O + k)[1], hgm, k, N0 + k)
                tail(l, 1, *q0(l, U_O + KD))

                ffn(l, 1)

        @block.tensor
        def _(pe):
            pe.sem_inc(unit_done, RING)

            def products(dst, tiles, first, last):
                for i, (sh, sl, mh, ml) in enumerate(tiles):
                    f, z = first and i == 0, last and i == len(tiles) - 1
                    pe.matmul(dst, sh, mh, start=f, stop=False)
                    pe.matmul(dst, sh, ml, start=False, stop=False)
                    ins = pe.matmul(dst, sl, mh, start=False, stop=z)
                return ins

            def wtile(s, i):
                return w_hi[:, s, i * P:(i + 1) * P], w_lo[:, s, i * P:(i + 1) * P]

            def in_part(s, dst, tok):
                return products(dst[:, tok], [(*wtile(s, k), x_hi[:, k, tok], x_lo[:, k, tok]) for k in range(KD)],
                                True, True)

            def in_unit(q, s, dst):
                pe.wait_ge(lo_ready, U(q, s) + (RING + 1))
                in_part(s, dst, slice(0, S)).then_inc(unit_done, 1)

            def out_unit(q, s, n, b, first, last):
                for i in range(2):
                    ins = products(bank[2 * b + i][:], [(a_hi[:, s, b * P:(b + 1) * P], a_lo[:, s, b * P:(b + 1) * P],
                                                         w_hi[:, s, i * S:i * S + S], w_lo[:, s, i * S:i * S + S])],
                                   first, last)
                return ins

            def xpose(l, n, b):
                pe.wait_ge(y_ready, l * 12 + (4 * n + b + 1 + C_Y))
                for i in range(2):
                    for k in range(4):
                        ins = pe.transpose(bank[2 * b + i][:, k * P:(k + 1) * P],
                                           res[:, b, (4 * i + k) * P:(4 * i + k + 1) * P], ident[:])
                    ins.then_inc(xpose_done, 1)

            def projection(l, n, rel, N0, K, banks01_free):
                q, s = q0(l, rel)

                def ready(k, q, s):
                    pe.wait_ge(lo_ready, U(q, s) + (RING + 1))
                    pe.wait_ge(alo_ready, N0 + k + 1)

                def whole(k, q, s, first=False):
                    ready(k, q, s)
                    for b in (2, 3, 0, 1):
                        if first and b == 0:
                            banks01_free()
                        ins = out_unit(q, s, N0, b, first, False)
                    ins.then_inc(unit_done, 1)

                whole(0, q, s, True)
                lead = (K - 4) % 4 or 4
                for k in range(1, lead):
                    whole(k, *adv(q, s, k))
                if K - 4 - lead:
                    with pe.Fori(0, (K - 4 - lead) // 4) as it:
                        for i in range(4):
                            whole(it * 4 + (lead + i), *adv(q + it, s, lead + i))
                for b in range(NB):
                    for k in range(K - 4, K):
                        qq, ss = adv(q, s, k)
                        if b == 0:
                            ready(k, qq, ss)
                        ins = out_unit(qq, ss, N0, b, False, k == K - 1)
                        if b == NB - 1:
                            ins.then_inc(unit_done, 1)
                    if b < NB - 1:
                        ins.then_inc(blk_done, 1)
                    if b > 0:
                        xpose(l, n, b - 1)
                if n == 2:
                    xpose(l, n, 3)
                    return
                pe.wait_ge(xlo_ready, l * 24 + (8 * n + KD + 6))
                for i in range(2):
                    qq, ss = adv(q, s, K + i)
                    pe.wait_ge(lo_ready, U(qq, ss) + (RING + 1))
                    in_part(ss, bank[i], PART[0])
                    if i == 0:
                        xpose(l, n, 3)
                x_ready(l, n + 1)
                for i in range(2):
                    in_part(adv(q, s, K + i)[1], bank[i], PART[1]).then_inc(unit_done, 1)

            def x_ready(l, n):
                pe.wait_ge(xlo_ready, l * 24 + (8 * n + KD))

            def ffn(l, f):
                q, s = q0(l, U_FFN[f])

                def pair(it, t):
                    pe.wait_ge(hmul_done, l * (2 * KF) + it * 2 + (f * KF + t + 1))
                    in_unit(*adv(q + it, s, 2 * t), bank[2 * t])
                    in_unit(*adv(q + it, s, 2 * t + 1), bank[2 * t + 1])

                if f == 0:
                    x_ready(l, 0)
                    pair(0, 0)
                pair(0, 1)
                with pe.Fori(1, KF // 2) as it:
                    pair(it, 0)
                    pair(it, 1)
                projection(l, 2 * f, U_FFN[f] + 2 * KF, l * (2 * KF + KD) + f * (KF + KD), KF,
                           lambda: pe.wait_ge(hmul_done, l * (2 * KF) + (f * KF + KF + C_HMUL)))

            def gn_mean(l, g):
                pe.wait_ge(conv_done, l * KD + g + 1)
                pe.matmul(bank[6][:], avg[:], conv_out(g), start=True, stop=True).then_inc(mean_done, 1)

            def gn_var(l, g):
                pe.wait_ge(sq_done, l * KD + g + 1)
                pe.matmul(bank[7][:], avg[:], gsq, start=True, stop=True).then_inc(var_done, 1)

            pe.wait_ge(consts, 4)
            with pe.Fori(0, L) as l:
                ffn(l, 0)

                def c_group(it, first):
                    q, s = q0(l, U_C)
                    for i in range(first, 4):
                        if i % 2 == 0:
                            pe.wait_ge(cmul_done, l * KD + it * 2 + (i // 2 + 1))
                        in_unit(*adv(q + it, s, i), bank[i])

                c_group(0, 2)
                with pe.Fori(1, 4) as it:
                    c_group(it, 0)

                def rg_group(it, n):
                    q, s = q0(l, U_RG)
                    for i in range(n):
                        if i % 2 == 0:
                            pe.wait_ge(cmul_done, l * KD + (KD - 1 + i // 2 + C_CMUL))
                        pe.wait_ge(gelu_done, l * KR + it * 4 + (i + 1))
                        in_unit(*adv(q + it, s, i), bank[i])

                with pe.Fori(0, 2) as it:
                    rg_group(it, 4)
                rg_group(2, 3)

                for i, (kind, j) in enumerate(R_UNITS):
                    q, s = q0(l, U_R + i)
                    if kind == "rx":
                        pe.wait_ge(rx_done, l * KR + (j + 1))
                        in_unit(q, s, bank[4 + j % 2])
                        continue
                    if kind == "bda":
                        if j < 2:
                            pe.wait_ge(gelu_done, l * KR + (KR + C_GELU))
                        else:
                            pe.wait_ge(ra_done, l * (KR * 5) + (5 * (j // 2 * 2 - 2) + 2 * (j % 2 + 1) + C_RA * 5))
                        pe.wait_ge(rclo_ready, l * KR + min(j + 2, KR))
                    pe.wait_ge(lo_ready, U(q, s) + (RING + 1))
                    near = [t for t in (j - 1, j, j + 1) if 0 <= t < KR]
                    products(bank[(0 if kind == "bda" else 2) + j % 2][:],
                             [(*wtile(s, t - j + 1), a_hi[:, t % 4], a_lo[:, t % 4]) for t in near], True, True
                             ).then_inc(unit_done, 1)

                def g_group(it):
                    q, s = q0(l, U_G)
                    for i in range(4):
                        if i == 2:
                            pe.wait_ge(ra_done, l * (KR * 5) + (5 * (KR - 1) + 2 + C_RA * 5))
                        pe.wait_ge(gate_done, l * (2 * KD) + it * 4 + (i + 1))
                        in_unit(*adv(q + it, s, i), bank[G_BANK[i]])
                        if i == 0:
                            gn_mean(l, it)
                        if i == 2:
                            gn_var(l, it)

                with pe.Fori(0, 4) as it:
                    g_group(it)

                def yr_tile(it, ff, first=False):
                    q, s = q0(l, U_YR)
                    pe.wait_ge(mr_done, l * KD + it * 2 + (ff + 1))
                    for i, (k0, k1) in enumerate(YR_SPLIT):
                        qq, ss = adv(q + it, s, 2 * ff + i)
                        pe.wait_ge(lo_ready, U(qq, ss) + (RING + 1))
                        for k in range(k0, k1):
                            if first:
                                pe.wait_ge(hs_lo, l * KR + (k + 1))
                            ins = products(bank[2 + ff][:], [(*wtile(ss, k - k0), *hg_pair(YR_ORDER[k]))],
                                           k == 0, k == KR - 1)
                        ins.then_inc(unit_done, 1)
                        if i == 0:
                            (gn_mean, gn_var)[ff](l, it + 4)

                yr_tile(0, 0, True)
                yr_tile(0, 1)
                with pe.Fori(1, KD // 2) as it:
                    yr_tile(it, 0)
                    yr_tile(it, 1)

                def yc_tile(q, s, i, n, first=False):
                    pe.wait_ge(m_done, n)
                    qq, ss = adv(q, s, i)
                    pe.wait_ge(lo_ready, U(qq, ss) + (RING + 1))
                    for k in range(KD):
                        if first:
                            pe.wait_ge(cs_lo, l * KD + (k + 1))
                        ins = products(bank[i % 2][:], [(*wtile(ss, k), *c_pair(k))], k == 0, k == KD - 1)
                    ins.then_inc(unit_done, 1)

                q, s = q0(l, U_YC)
                pe.wait_ge(gate_done, l * (2 * KD) + (2 * KD + C_GATE))
                for i in range(4):
                    yc_tile(q, s, i, l * KD + (i + 1), i == 0)
                for i in range(4):
                    yc_tile(q + 1, s, i, l * KD + (i + 5))

                projection(l, 1, U_O, l * (2 * KF + KD) + KF, KD,
                           lambda: pe.wait_ge(m_done, l * KD + (KD + C_M)))

                ffn(l, 1)


def _units(np, i):
    W = np.zeros((L, UPL, P, UW), np.float32)

    def tiles(w, cols):
        K = w.shape[0] // P
        return [w[:, c:c + P].reshape(K, P, P).transpose(1, 0, 2).reshape(P, K * P) for c in cols]

    for l in range(L):
        for f, n in enumerate(("ffn1", "ffn2")):
            gu, down = i[f"{n}_w_gu"][l], i[f"{n}_w_down"][l]
            b = U_FFN[f]
            for t in range(KF):
                W[l, b + 2 * t], W[l, b + 2 * t + 1] = tiles(gu, (t * P, DFF + t * P))
            W[l, b + 2 * KF:b + 3 * KF] = down.reshape(KF, P, D)
        w = i["mix_w_in"][l]
        oc, og = 0, D
        orx, org = 2 * D, 2 * D + DRNN
        ogc, ogr = 2 * D + 2 * DRNN, 3 * D + 2 * DRNN
        for j in range(KD):
            W[l, U_C + 2 * j], W[l, U_C + 2 * j + 1] = tiles(w, (oc + j * P, og + j * P))
            W[l, U_G + 2 * j], W[l, U_G + 2 * j + 1] = tiles(w, (ogc + j * P, ogr + j * P))
        for j in range(KR):
            W[l, U_RG + j] = tiles(w, (org + j * P,))[0]
        band = {}
        for kind, name in (("bda", "rnn_w_a"), ("bdx", "rnn_w_x")):
            m = np.zeros((DRNN, DRNN), np.float32)
            for b in range(DRNN // RB):
                m[b * RB:(b + 1) * RB, b * RB:(b + 1) * RB] = i[name][l, b]
            band[kind] = m
        for n, (kind, j) in enumerate(R_UNITS):
            if kind == "rx":
                W[l, U_R + n] = tiles(w, (orx + j * P,))[0]
                continue
            for t in (j - 1, j, j + 1):
                if 0 <= t < KR:
                    W[l, U_R + n, :, (t - j + 1) * P:(t - j + 2) * P] = \
                        band[kind][t * P:(t + 1) * P, j * P:(j + 1) * P]
        for f in range(KD):
            t = tiles(i["rnn_w_proj"][l], (f * P,))[0].reshape(P, KR, P)[:, YR_ORDER].reshape(P, KR * P)
            for n, (k0, k1) in enumerate(YR_SPLIT):
                W[l, U_YR + 2 * f + n, :, 0:(k1 - k0) * P] = t[:, k0 * P:k1 * P]
            W[l, U_YC + f] = tiles(i["conv_w_proj"][l], (f * P,))[0]
        W[l, U_O:U_O + KD] = i["mix_w_out"][l].reshape(KD, P, D)
    return W.reshape(L * UPL, P, UW)


def _params(np, i):
    A = np.zeros((P, L, NPAR), np.float32)

    def put(name, l, v, at=0, step=1):
        v = v.reshape(v.shape[0] // P, P, -1).transpose(1, 0, 2)
        n = v.shape[1] * v.shape[2]
        A[:, l, PC[name] + at:PC[name] + at + step * (n - 1) + 1:step] = v.reshape(P, n)

    for l in range(L):
        b = i["mix_b_in"][l]
        put("b_c", l, b[0:D], 0, 2)
        put("b_c", l, b[D:2 * D], 1, 2)
        o = 2 * D
        put("b_rx", l, b[o:o + DRNN])
        put("b_rg", l, b[o + DRNN:o + 2 * DRNN])
        o += 2 * DRNN
        put("b_g", l, b[o:o + D], 0, 2)
        put("b_g", l, b[o + D:o + 2 * D], 1, 2)
        put("cw", l, i["conv_dw_w"][l].T)
        put("cb", l, i["conv_dw_b"][l])
        put("gg", l, i["conv_gn_g"][l])
        put("gb", l, i["conv_gn_b"][l])
        put("rw", l, i["rnn_conv_w"][l].T)
        put("rb", l, i["rnn_conv_b"][l])
        put("ba", l, i["rnn_b_a"][l])
        put("bx", l, i["rnn_b_x"][l])
        put("lam", l, i["rnn_lambda"][l])
    return A.reshape(P, L * NPAR)


def kernel(**inputs):
    import numpy as np
    import concourse.bacc as bacc
    from concourse.bass_utils import run_bass_kernel_spmd

    i = {k: np.asarray(v) for k, v in inputs.items()}
    x = i["x"].reshape(S, D)
    lnp = np.empty((L * 3, P, 2, D), np.float32)
    for l in range(L):
        for n in range(3):
            lnp[3 * l + n, :, 0], lnp[3 * l + n, :, 1] = i[f"ln{n + 1}_g"][l], i[f"ln{n + 1}_b"][l]
    arrays = {
        "wst": _units(np, i),
        "xT": np.ascontiguousarray(x.T.reshape(KD, P, S).transpose(1, 0, 2)),
        "xtok": np.ascontiguousarray(x),
        "par": _params(np, i),
        "lnp": lnp,
    }
    nc = bacc.Bacc("TRN2", target_bir_lowering=False, num_devices=1)
    args = [nc.dram_tensor(n, a.shape, F32, kind="ExternalInput").ap() for n, a in arrays.items()]
    out = nc.dram_tensor("out", (S, D), F32, kind="ExternalOutput").ap()
    trunk(nc, *args, out)
    r = run_bass_kernel_spmd(nc, [arrays], core_ids=[0])
    return r.results[0]["out"].reshape(1, S, D)
```

```python
import math

import concourse.bass as bass
from concourse import mybir

F32 = mybir.dt.float32
F32R = mybir.dt.float32r
ALU = mybir.AluOpType
ACT = mybir.ActivationFunctionType

P = 128
RING = 4
AHEAD = 3
EPS = 1e-5

L, S, D = 2, 512, 1024
DFF, DRNN = 2816, 1408
TAPS, RTAPS = 31, 4
KD, KF, KR = D // P, DFF // P, DRNN // P
NB = S // P
RB = DRNN // 16
ALPHA = (2 * L) ** 0.25
UW = 1024

FFN_UNITS = 2 * KF + KF
MIX = FFN_UNITS
U_C, U_RG = MIX, MIX + 2 * KD
U_R = U_RG + KR
G_EARLY = 3
U_G = U_R + 3 * KR + G_EARLY
U_YR = U_G + 2 * KD - G_EARLY
U_YC = U_YR + 2 * KD
U_O = U_YC + KD
U_FFN = (0, U_O + KD)
UPL = U_FFN[1] + FFN_UNITS
assert UPL % RING == 0
HALVES = (slice(0, S // 2), slice(S // 2, S))
N_LAM = 17

R_GROUPS = [[("rx", 0), ("rx", 1), ("rx", 2)]]
for _p in range(0, KR, 2):
    R_GROUPS.append([])
    for _j in (_p, _p + 1):
        if _j < KR:
            R_GROUPS[-1] += [("rx", _j + 3) if _j + 3 < KR else ("g", _j + 3 - KR), ("bda", _j), ("bdx", _j)]
R_UNITS = [u for g in R_GROUPS for u in g]
assert len(R_UNITS) == U_G - U_R
YR_ORDER = [7, 8, 9, 10, 0, 1, 2, 3, 4, 5, 6]
YR_SPLIT = [(0, 6), (6, KR)]
HG_SLOT = {7: 1, 8: 0, 9: 2, 10: 3}
C_SLOT = {0: 1, 1: 0, 2: 3}

VTAPS = TAPS - 2
TAPS_BY = {U_C - 1: 0}
for _i in range(2 * KD):
    TAPS_BY[U_C + _i] = max(0, 72 * (_i - 2) // (2 * KD - 3))
for _i in range(KR):
    TAPS_BY[U_RG + _i] = 72 + 59 * (_i + 1) // KR
for _i in range(U_G - U_R + 1):
    TAPS_BY[U_R + _i] = min(131 + 2 * (_i + 1), 137 + 8 * (max(_i, 2) - 2) // 6, 5 * VTAPS)
for _i in range(4):
    TAPS_BY[U_G - 4 + _i] = 5 * VTAPS + (2, 4, 5, 6)[_i]
for _i in range(U_YR - U_G):
    TAPS_BY[U_G + _i] = 5 * VTAPS + (10, 14, 17, 21, 25, 29, 33, 38, 42, 46, 50, 54, 57)[_i]
for _i in range(2 * KD):
    TAPS_BY[U_YR + _i] = min(TAPS_BY[U_YR - 1] + 10 * _i // 3, KD * VTAPS)
INIT_AT = {U_C + 3: 0, U_G - 5: 5}
for _rel in range(U_C, U_YR + 2 * KD):
    for _c in (1, 2, 3, 4, 6, 7):
        if TAPS_BY[_rel - 1] < _c * VTAPS <= TAPS_BY[_rel]:
            INIT_AT[_rel] = _c
assert len(INIT_AT) == KD and TAPS_BY[U_YR + 2 * KD - 1] == KD * VTAPS

PC = {}
_n = 0
for _name, _w in (("b_c", 2 * KD), ("b_rg", KR), ("b_rx", KR), ("b_g", 2 * KD), ("cw", KD * TAPS), ("cb", KD),
                  ("gg", KD), ("gb", KD), ("rw", KR * RTAPS), ("rb", KR), ("ba", KR), ("bx", KR), ("lam", KR)):
    PC[_name] = _n
    _n += _w
NPAR = _n
SQ_UP = 2.0 ** 60


def adv(q, s, d):
    return q + (s + d) // RING, (s + d) % RING


def trunk(nc, wst, xtok, par, lnp, out):
    sb, at = nc.alloc_sbuf_tensor, nc.alloc_sbuf_tensor_at
    w_raw = sb("w_raw", [P, RING, UW], F32)
    w_hi = sb("w_hi", [P, RING, UW], F32R)
    w_lo = sb("w_lo", [P, RING, UW], F32R)
    x_hi = sb("x_hi", [P, KD, S], F32R)
    x_lo = sb("x_lo", [P, KD, S], F32R)
    res = sb("res", [P, NB, D], F32)
    a_hi = sb("a_hi", [P, RING, S], F32R)
    a_lo = sb("a_lo", [P, RING, S], F32R)
    pr = sb("pr", [P, L * NPAR], F32)
    sp8 = sb("sp8", [P, 2, L * KR], F32)
    lt = sb("lt", [P, 4, KR], F32)
    ident = sb("ident", [P, P], F32)
    avg = sb("avg", [P, P], F32)
    lns = sb("lns", [P, 2, 8], F32)
    epsb = sb("epsb", [P, 1], F32)
    mhalf = sb("mhalf", [P, 1], F32)

    sb("arena", [P, 23040], F32)
    A0 = nc.sbuf_base - 23040 * 4
    gates = at("gates", [P, 2 * KD, S], F32, offset=A0)
    hgm = at("hgm", [P, KR, S], F32, offset=A0 + 32768)
    cpad = at("cpad", [P, KD, TAPS - 1 + S], F32, offset=A0 + 55296)
    ct = at("ct", [P, 6, S], F32, offset=A0 + 72640)
    rxp = at("rxp", [P, 2, RTAPS - 1 + S], F32, offset=A0 + 84928)
    tx = at("tx", [P, 1, S], F32, offset=A0 + 89056)
    h = at("h", [P, KF, S], F32, offset=A0)
    sg = at("sg", [P, 1, S], F32, offset=A0 + 45056)
    yb = at("yb", [P, 2, D], F32, offset=A0 + 47104)
    gb = at("gb", [P, 2, D], F32, offset=A0 + 55296)
    sq = at("sq", [P, D], F32, offset=A0 + 63488)
    yg = at("yg", [P, D], F32, offset=A0 + 67584)

    gsq, grs = ct[:, 2], ct[:, 3]
    sgc = tx[:, 0]
    rcf = [gates[:, 11], gates[:, 12], gates[:, 13], gates[:, 14], hgm[:, 8]]
    accs = [(hgm[:, 9], hgm[:, 10]), (hgm[:, 7], hgm[:, 8]), (hgm[:, 9], hgm[:, 10]), (hgm[:, 7], hgm[:, 8]),
            (hgm[:, 9], hgm[:, 10]), (gates[:, 12], gates[:, 13]), (ct[:, 0], ct[:, 1]), (ct[:, 4], ct[:, 5])]
    RT = [[gates[:, 15], tx[:, 0], ct[:, 0], ct[:, 1]], [ct[:, 2], ct[:, 3], ct[:, 4], ct[:, 5]]]

    bank = [nc.alloc_psum_tensor(f"bank{i}", [P, S], F32) for i in range(8)]

    sem = nc.alloc_semaphore
    raw_landed = [sem(f"raw_landed{i}") for i in range(RING)]
    res_landed = [sem(f"res_landed{b}") for b in range(NB)]
    par_landed, gb_landed = sem("par_landed"), sem("gb_landed")
    out_written = sem("out_written")
    consts, eps_ready = sem("consts"), sem("eps_ready")
    settled = sem("settled")
    hi_ready, lo_ready, unit_done = sem("hi_ready"), sem("lo_ready"), sem("unit_done")
    lam_act, lam_dve = sem("lam_act"), sem("lam_dve")
    silu_done, hmul_done = sem("silu_done"), sem("hmul_done")
    ahi_ready, alo_ready = sem("ahi_ready"), sem("alo_ready")
    blk_done, ln_chain, rstd_ready, y_ready = sem("blk_done"), sem("ln_chain"), sem("rstd_ready"), sem("y_ready")
    lnsq_done, lnvar_done = sem("lnsq_done"), sem("lnvar_done")
    xpose_done, xhi_ready, xlo_ready = sem("xpose_done"), sem("xhi_ready"), sem("xlo_ready")
    pads_ready = sem("pads_ready")
    csig_done, cmul_done = sem("csig_done"), sem("cmul_done")
    init_done, tap_done, conv_done = sem("init_done"), sem("tap_done"), sem("conv_done")
    mean_done, xc_done, sq_done, var_done = sem("mean_done"), sem("xc_done"), sem("sq_done"), sem("var_done")
    gln_done, grs_done, gy_done, gn_done = sem("gln_done"), sem("grs_done"), sem("gy_done"), sem("gn_done")
    gelu_done, rx_done, rtap_done, rc_done = sem("gelu_done"), sem("rx_done"), sem("rtap_done"), sem("rc_done")
    rchi_ready, rclo_ready = sem("rchi_ready"), sem("rclo_ready")
    ra_done, rs_done, rv_done, ru_done, hg_done = (sem(x) for x in ("ra_done", "rs_done", "rv_done", "ru_done", "hg_done"))
    gate_done = sem("gate_done")
    cs_hi, cs_lo, hs_hi, hs_lo = (sem(x) for x in ("cs_hi", "cs_lo", "hs_hi", "hs_lo"))
    mr_done, mc_done, m_done = sem("mr_done"), sem("mc_done"), sem("m_done")

    C_HMUL, C_CMUL, C_GELU, C_RX, C_RA, C_GATE, C_M, C_MR, C_Y = 2, 2, 4, 2, 2, 4, 2, 2, NB

    def U(q, s):
        return q * RING + s

    def q0(l, rel):
        return l * (UPL // RING) + rel // RING, rel % RING

    def one(t, i):
        return t[:, bass.ds(i, 1)].rearrange("p a n -> p (a n)")

    def col(name, l, i):
        return pr[:, bass.ds(l * NPAR + (i + PC[name]), 1)]

    def conv_out(g):
        return cpad[:, bass.ds(g, 1), TAPS - 1:].rearrange("p a n -> p (a n)")

    def hg_pair(j):
        return (a_hi[:, HG_SLOT[j]], a_lo[:, HG_SLOT[j]]) if j in HG_SLOT else (x_hi[:, j], x_lo[:, j])

    def c_pair(j):
        return (a_hi[:, C_SLOT[j]], a_lo[:, C_SLOT[j]]) if j in C_SLOT else (x_hi[:, j], x_lo[:, j])

    def unit_cols(rel):
        if U_R <= rel < U_G:
            return 3 * P if R_UNITS[rel - U_R][0] in ("bda", "bdx") else UW
        if U_YR <= rel < U_YC:
            k0, k1 = YR_SPLIT[(rel - U_YR) % 2]
            return (k1 - k0) * P
        return UW

    def r_done(l, kind, j):
        return l * UPL + (U_R + R_UNITS.index((kind, j)) + RING + 1)

    def done(l, rel):
        return l * UPL + (rel + RING + 1)

    def g_rel(i):
        return U_R + R_UNITS.index(("g", i)) if i < G_EARLY else U_G + i - G_EARLY

    def g_bank(i):
        return bank[6 + i % 2] if i in (2, 3) else bank[(5, 4, 1, 3)[i % 4]]

    def f32(ap):
        return ap.bitcast(F32)

    def settle(eng):
        eng.sem_inc(settled, 1)

    with nc.Block() as block:

        @block.sync
        def _(sp):
            def load(q, s, cols=UW):
                sp.wait_ge(lo_ready, U(q, s) + 1)
                sp.dma_start(w_raw[:, s, 0:cols],
                             wst[bass.ds(U(q, s), 1), :, 0:cols].rearrange("u p n -> (u p) n")
                             ).then_inc(raw_landed[s], 16)

            def loads(q, s, n):
                with sp.Fori(0, n // RING) as it:
                    for i in range(RING):
                        load(*adv(q + it, s, i))
                for i in range(n // RING * RING, n):
                    load(*adv(q, s, i))

            for b in range(2):
                sp.dma_start(res[:, b], xtok[b * P:(b + 1) * P, :]).then_inc(res_landed[b], 16)
            with sp.Fori(0, L) as l:
                loads(*q0(l, 0), U_R)
                for rel in range(U_R, U_G):
                    load(*q0(l, rel), unit_cols(rel))
                loads(*q0(l, U_G), U_YR - U_G)
                with sp.Fori(0, KD // 2) as it:
                    qy, sy = q0(l, U_YR)
                    for i in range(4):
                        load(*adv(qy + it, sy, i), unit_cols(U_YR + i))
                loads(*q0(l, U_YC), UPL - U_YC)
            for s in range(AHEAD - 1):
                sp.wait_ge(lo_ready, L * UPL + s + 1)
                sp.dma_start(w_raw[:, s], wst[s]).then_inc(raw_landed[s], 16)
            for b in range(NB):
                sp.wait_ge(y_ready, C_Y + (L * 3 - 1) * NB + b + 1)
                sp.dma_start(out[b * P:(b + 1) * P, :], res[:, b]).then_inc(out_written, 16)
            sp.wait_ge(out_written, 16 * NB)

        @block.gpsimd
        def _(pool):
            pool.memset(ident[:], 0.0).then_inc(consts, 1)
            pool.memset(avg[:], 1.0 / P).then_inc(consts, 1)
            pool.memset(mhalf[:], -0.5).then_inc(consts, 1)
            pool.wait_ge(consts, 3)
            pool.affine_select(out=ident[:], in_=ident[:], compare_op=ALU.not_equal, fill=1.0, base=0,
                               pattern=[[-1, P]], channel_multiplier=1).then_inc(consts, 1)
            pool.wait_ge(consts, 4)
            for b in range(NB):
                pool.wait_ge(res_landed[b], 16)
                pool.sem_inc(y_ready, 1)
            pool.dma_start(pr[:], par).then_inc(par_landed, 16)

            def layer_norm(l, n, ready):
                ready()
                pool.dma_start(gb[:], lnp[bass.ds(l * 3 + n, 1)].rearrange("a p c d -> p (a c) d")
                               ).then_inc(gb_landed, 16)
                for b in range(NB):
                    X, st = l * 12 + (4 * n + b), lns[:, b % 2]
                    if b >= 2:
                        pool.wait_ge(y_ready, X + (C_Y - 1))
                    pool.wait_ge(lnsq_done, X + 1)
                    settle(pool)
                    pool.tensor_scalar(st[:, 4:5], st[:, 3:4], 1.0 / D, EPS / ALPHA ** 2, ALU.mult, ALU.add
                                       ).then_inc(lnvar_done, 1)
                    pool.wait_ge(lnvar_done, X + 1)
                    pool.tensor_tensor(st[:, 5:6], st[:, 4:5], mhalf[:], ALU.pow).then_inc(rstd_ready, 1)

            with pool.Fori(0, L) as l:
                layer_norm(l, 0, lambda: pool.wait_ge(y_ready, l * 12 + C_Y))
                layer_norm(l, 1, lambda: pool.wait_ge(cs_lo, l * KD + KD))
                layer_norm(l, 2, lambda: pool.wait_ge(y_ready, l * 12 + (C_Y + 8)))

        @block.scalar
        def _(act):
            act.wait_ge(consts, 3)
            act.activation(lns[:, 0, 6:7], mhalf[:], ACT.Copy)
            act.wait_ge(res_landed[0], 16)
            for b in range(2, NB):
                act.dma_start(res[:, b], xtok[b * P:(b + 1) * P, :]).then_inc(res_landed[b], 16)
            act.sem_inc(gelu_done, C_GELU)
            act.sem_inc(rx_done, C_RX)
            act.sem_inc(ra_done, C_RA * 5)
            act.sem_inc(gate_done, C_GATE)

            def split(q, s, cols=UW):
                act.wait_ge(raw_landed[s], q * 16 + 16)
                act.wait_ge(unit_done, U(q, s) + 1)
                act.activation(w_hi[:, s, 0:cols], w_raw[:, s, 0:cols], ACT.Copy).then_inc(hi_ready, 1)

            def asplit(q, s, src, k, n):
                act.wait_ge(unit_done, U(q, s) + 1)
                act.activation(a_hi[:, s], one(src, k), ACT.Copy).then_inc(ahi_ready, 1)

            def xt(l, n, b):
                for i in range(2):
                    act.wait_ge(xpose_done, l * 24 + (KD + 8 * n + 2 * b + i + 1))
                    act.activation(x_hi[:, 4 * i:4 * i + 4, b * P:(b + 1) * P],
                                   bank[2 * b + i][:].rearrange("p (k n) -> p k n", k=4), ACT.Copy
                                   ).then_inc(xhi_ready, 1)

            def ln_square(l, n, b):
                X, st = l * 12 + (4 * n + b), lns[:, b % 2]
                act.wait_ge(ln_chain, X * 4 + 3)
                if b:
                    act.wait_ge(lnsq_done, X)
                act.activation(sq[:], yb[:, b % 2], ACT.Square, bias=st[:, 2:3], accum_out=st[:, 3:4]
                               ).then_inc(lnsq_done, 1)

            def tail(l, n, q, s):
                ln_square(l, n, 0)
                ln_square(l, n, 1)
                xt(l, n, 0)
                ln_square(l, n, 2)
                xt(l, n, 1)
                split(*adv(q, s, 0))
                split(*adv(q, s, 1))
                ln_square(l, n, 3)

            def resume(l, n, q, s):
                split(*adv(q, s, 2))
                xt(l, n, 2)
                xt(l, n, 3)

            def ffn(l, f):
                q, s = q0(l, U_FFN[f])

                def pair(q, s, t, down):
                    T = l * (2 * KF) + (f * KF + t)
                    for i in range(2):
                        split(*adv(q, s, AHEAD + i))
                        if down[i] is not None:
                            asplit(*adv(q, s, AHEAD + i), h, down[i], None)
                    act.wait_ge(unit_done, U(q, s) + (RING + 1))
                    act.wait_ge(hmul_done, T + C_HMUL)
                    act.activation(sg[:, 0], bank[down[2]][:], ACT.Silu).then_inc(silu_done, 1)

                with act.Fori(0, KF // 2 - 1) as it:
                    pair(*adv(q + it, s, 0), it * 2, (None, None, 0))
                    pair(*adv(q + it, s, 2), it * 2 + 1, (None, None, 2))
                if f == 0:
                    act.wait_ge(lam_dve, l * N_LAM + 1)
                    act.activation(lt[:, 1], lt[:, 0], ACT.Exp, scale=-1.0).then_inc(lam_act, 1)
                pair(*adv(q, s, 2 * KF - 4), KF - 2, (None, 0, 0))
                pair(*adv(q, s, 2 * KF - 2), KF - 1, (1, 2, 2))
                qd, sd = adv(q, s, 2 * KF)
                for k in (0, 1):
                    split(*adv(qd, sd, k + AHEAD))
                    asplit(*adv(qd, sd, k + AHEAD), h, k + AHEAD, None)
                with act.Fori(0, 4) as it:
                    for i in range(4):
                        split(*adv(qd + it, sd, 2 + i + AHEAD))
                        asplit(*adv(qd + it, sd, 2 + i + AHEAD), h, it * 4 + (2 + i + AHEAD), None)
                split(*adv(qd, sd, 18 + AHEAD))
                asplit(*adv(qd, sd, 18 + AHEAD), h, 18 + AHEAD, None)
                tail(l, 2 * f, *adv(qd, sd, KF))
                if f == 0:
                    resume(l, 0, *adv(qd, sd, KF))

            def gn_square(l, g):
                act.wait_ge(xc_done, l * KD + g + 1)
                act.activation(gsq, conv_out(g), ACT.Square).then_inc(sq_done, 1)

            def gn_rstd(l, g):
                act.wait_ge(var_done, l * KD + g + 1)
                act.activation(grs, bank[7][:], ACT.Ln, bias=epsb[:]).then_inc(gln_done, 1)
                act.wait_ge(gln_done, l * KD + g + 1)
                act.activation(grs, grs, ACT.Exp, scale=-0.5).then_inc(grs_done, 1)

            def gn_silu(l, g):
                act.wait_ge(gy_done, l * KD + g + 1)
                act.activation(conv_out(g), conv_out(g), ACT.Silu, bias=col("gb", l, g), scale=col("gg", l, g)
                               ).then_inc(gn_done, 1)

            def hg_hi(l, j):
                act.activation(hg_pair(j)[0], hgm[:, j], ACT.Copy).then_inc(hs_hi, 1)

            def c_hi(l, j):
                act.wait_ge(gn_done, l * KD + j + 1)
                act.activation(c_pair(j)[0], conv_out(j), ACT.Copy).then_inc(cs_hi, 1)

            act.wait_ge(eps_ready, 1)
            xt(0, -1, 0)
            for s in range(AHEAD - 1):
                act.wait_ge(raw_landed[s], 16)
                act.activation(w_hi[:, s], w_raw[:, s], ACT.Copy).then_inc(hi_ready, 1)
                if s == 0:
                    xt(0, -1, 1)

            with act.Fori(0, L) as l:
                resume(l, -1, *q0(l, 0))
                ffn(l, 0)

                def ahead(rel):
                    split(*q0(l, rel + AHEAD), unit_cols(rel + AHEAD))

                def conv_init(rel):
                    if rel not in INIT_AT:
                        return
                    c = INIT_AT[rel]
                    act.wait_ge(cmul_done, l * KD + (c + 1 + C_CMUL))
                    if c == 0:
                        act.wait_ge(pads_ready, l * 2 + 1)
                    elif c == 5:
                        act.wait_ge(rv_done, l * (KR * 2) + 14)
                    elif c == 6:
                        act.wait_ge(hg_done, l * KR + KR)
                    elif c >= 2:
                        act.wait_ge(conv_done, l * KD + (c - 1))
                    act.activation(accs[c][0], cpad[:, c, 0:S], ACT.Identity, bias=col("cb", l, c),
                                   scale=col("cw", l, c * TAPS)).then_inc(init_done, 1)
                    act.activation(accs[c][1], cpad[:, c, 1:1 + S], ACT.Copy, scale=col("cw", l, c * TAPS + 1)
                                   ).then_inc(init_done, 1)

                def c_gate(j):
                    act.wait_ge(unit_done, done(l, U_C + 2 * j + 1))
                    act.wait_ge(cmul_done, l * KD + (j + C_CMUL))
                    act.activation(sgc, bank[2 * (j % 2) + 1][:], ACT.Sigmoid,
                                   bias=col("b_c", l, j * 2 + 1)).then_inc(csig_done, 1)

                for i in range(2 * KD):
                    ahead(U_C + i)
                    conv_init(U_C + i)
                    if i % 2 == 0 and i:
                        c_gate(i // 2 - 1)

                def rg_gelu(j):
                    act.wait_ge(unit_done, done(l, U_RG + j))
                    act.activation(gates[:, j], bank[j % 4][:], ACT.Gelu_apprx_tanh,
                                   bias=col("b_rg", l, j)).then_inc(gelu_done, 1)

                def norm_steps(i, g):
                    if i % 4 == 2:
                        gn_square(l, g)
                    if i % 4 == 3:
                        gn_rstd(l, g)

                for i in range(KR):
                    ahead(U_RG + i)
                    conv_init(U_RG + i)
                    if i == 0:
                        c_gate(KD - 1)
                    else:
                        rg_gelu(i - 1)
                    if i in (4, 8):
                        gn_silu(l, i // 4 - 1)
                    norm_steps(i, i // 4)

                def rx_evac(j):
                    act.wait_ge(unit_done, r_done(l, "rx", j))
                    act.wait_ge(pads_ready, l * 2 + 2)
                    if j >= 2:
                        act.wait_ge(rc_done, l * KR + (j - 1))
                    act.activation(rxp[:, j % 2, RTAPS - 1:], bank[4 + j % 2][:], ACT.Identity,
                                   bias=col("b_rx", l, j)).then_inc(rx_done, 1)

                def rc_hi(j):
                    act.wait_ge(rc_done, l * KR + (j + 1))
                    if j >= 4:
                        act.wait_ge(unit_done, r_done(l, "bdx", j - 3))
                    act.activation(a_hi[:, j % 4], rcf[j % 5], ACT.Copy).then_inc(rchi_ready, 1)

                def r_sigmoids(js):
                    for j in js:
                        r, i, a, v = RT[j % 2]
                        act.wait_ge(unit_done, r_done(l, "bdx", j))
                        pair = 2 * (j // 2 * 2 - 2) + (j % 2 + 1)
                        if j >= 2:
                            act.wait_ge(rv_done, l * (KR * 2) + (pair + 2))
                        act.activation(r, bank[j % 2][:], ACT.Sigmoid, bias=col("ba", l, j)).then_inc(ra_done, 1)
                        if j >= 2:
                            act.wait_ge(ru_done, l * (KR * 2) + pair)
                        act.activation(i, bank[2 + j % 2][:], ACT.Sigmoid, bias=col("bx", l, j)).then_inc(ra_done, 1)

                def r_exps(js, between=None):
                    n = l * (KR * 5) + (5 * js[0] + 2 * len(js) + C_RA * 5)
                    act.wait_ge(ra_done, n)
                    for m, j in enumerate(js):
                        r, i, a, v = RT[j % 2]
                        if j >= 2:
                            act.wait_ge(ru_done, l * (KR * 2) + (2 * (j // 2 * 2 - 2) + (j % 2 + 3)))
                        act.activation(a, r, ACT.Exp, scale=sp8[:, 1, bass.ds(l * KR + j, 1)]).then_inc(ra_done, 1)
                        act.wait_ge(ra_done, n + (3 * m + 1))
                        act.activation(v, a, ACT.Square).then_inc(ra_done, 1)
                        act.activation(r, r, ACT.Tanh, scale=sp8[:, 0, bass.ds(l * KR + j, 1)]).then_inc(ra_done, 1)
                        if m == 0 and between is not None:
                            rc_hi(between)

                def r_sqrts(js):
                    for j in js:
                        v = RT[j % 2][3]
                        act.wait_ge(rv_done, l * (KR * 2) + (2 * (js[-1] + 1) if j == js[0] else 2 * (j + 1)))
                        act.activation(v, v, ACT.Sqrt, scale=SQ_UP).then_inc(rs_done, 1)

                def gate(i):
                    act.wait_ge(unit_done, done(l, g_rel(i)))
                    act.wait_ge(hg_done, l * KR + min(i + 1, KR))
                    act.activation(gates[:, i], g_bank(i)[:], ACT.Sigmoid, bias=col("b_g", l, i)
                                   ).then_inc(gate_done, 1)

                rel = U_R
                for i in range(3):
                    ahead(rel + i)
                    conv_init(rel + i)
                    if i == 0:
                        rg_gelu(KR - 1)
                    else:
                        rx_evac(i - 1)
                    if i == 0:
                        gn_rstd(l, 2)
                    if i == 1:
                        gn_silu(l, 2)
                    if i == 2:
                        rc_hi(0)
                rel += 3
                for p in range(0, KR - 1, 2):
                    old = [p - 2, p - 1] if p else []
                    for i in range(6):
                        ahead(rel + i)
                        conv_init(rel + i)
                        if i == 0 and p == 0:
                            rc_hi(1)
                            rx_evac(2)
                        if i == 0:
                            r_sigmoids(old)
                        if i == 1:
                            if p + 3 < KR:
                                rx_evac(p + 3)
                            else:
                                gate(0)
                            if old:
                                r_exps(old, p + 2)
                            else:
                                rc_hi(p + 2)
                        if i == 3:
                            if old:
                                r_sqrts(old)
                            if p + 3 < KR:
                                rc_hi(p + 3)
                        if i == 4 and p + 4 < KR:
                            rx_evac(p + 4)
                    rel += 6
                old, last = [KR - 3, KR - 2], [KR - 1]
                for i in range(3):
                    ahead(rel + i)
                    if i == 0:
                        gate(1)
                        r_sigmoids(old)
                    if i == 1:
                        gate(2)
                        r_exps(old)
                    if i == 2:
                        r_sqrts(old)

                for i in range(G_EARLY, 2 * KD):
                    ahead(g_rel(i))
                    conv_init(g_rel(i))
                    if i == 3:
                        r_sigmoids(last)
                    else:
                        gate(i - 1)
                    if i == 4:
                        r_exps(last)
                    if i == 5:
                        r_sqrts(last)
                    if i == 12:
                        gn_silu(l, 3)
                    if i >= 8:
                        norm_steps(i, i // 4 + 1)
                    if i == 12:
                        for j in HG_SLOT:
                            hg_hi(l, j)

                act.wait_ge(unit_done, done(l, U_YR - 1))
                for j in range(KR - len(HG_SLOT)):
                    hg_hi(l, j)
                for i in range(2 * KD):
                    ahead(U_YR + i)
                    conv_init(U_YR + i)
                    if i == 0:
                        gate(2 * KD - 1)
                        gn_silu(l, 4)
                    if i == 15:
                        for j in C_SLOT:
                            c_hi(l, j)
                    if i % 4 == 0 and i > 3:
                        gn_square(l, i // 4 + 4)
                    if i % 4 == 1 and i > 4:
                        gn_rstd(l, i // 4 + 4)
                    if i % 4 == 2 and i > 4:
                        gn_silu(l, i // 4 + 4)

                act.wait_ge(unit_done, done(l, U_YC - 1))
                for j in range(3, KD):
                    c_hi(l, j)
                for i in range(KD):
                    ahead(U_YC + i)

                def o_tile(k):
                    act.wait_ge(m_done, l * KD + (k + 1 + C_M))
                    act.wait_ge(unit_done, done(l, U_O + (max(k - RING, -1) if k else -RING)))
                    act.activation(a_hi[:, q0(l, U_O + k)[1]], hgm[:, k], ACT.Copy).then_inc(ahi_ready, 1)

                for k in range(AHEAD):
                    o_tile(k)
                for k in range(AHEAD, KD):
                    split(*q0(l, U_O + k))
                    o_tile(k)
                tail(l, 1, *q0(l, U_O + KD))
                resume(l, 1, *q0(l, U_O + KD))

                ffn(l, 1)

        @block.vector
        def _(dve):
            dve.sem_inc(lo_ready, RING)
            dve.sem_inc(hmul_done, C_HMUL)
            dve.sem_inc(cmul_done, C_CMUL)
            dve.sem_inc(m_done, C_M)
            dve.sem_inc(mr_done, C_MR)

            def split(q, s, cols=UW):
                dve.wait_ge(hi_ready, U(q, s) + 1)
                dve.tensor_tensor(w_lo[:, s, 0:cols], w_raw[:, s, 0:cols], f32(w_hi[:, s, 0:cols]),
                                  ALU.subtract).then_inc(lo_ready, 1)

            def asplit(s, src, k, n):
                dve.wait_ge(ahi_ready, n + 1)
                dve.tensor_tensor(a_lo[:, s], one(src, k), f32(a_hi[:, s]), ALU.subtract).then_inc(alo_ready, 1)

            def ln_sums(l, n, b):
                X = l * 12 + (4 * n + b)
                y, st = yb[:, b % 2], lns[:, b % 2]
                gain = (1.0 if n == 1 else 0.5) / ALPHA
                if b < NB - 1:
                    dve.wait_ge(blk_done, l * 9 + (3 * n + b + 1))
                else:
                    dve.wait_ge(unit_done, l * UPL + ((MIX, U_FFN[1], UPL)[n] + RING))
                if b >= 2:
                    dve.wait_ge(y_ready, X + (C_Y - 1))
                for i in range(2):
                    cols = slice(S * i, S * i + S)
                    dve.scalar_tensor_tensor(y[:, cols], bank[2 * b + i][:], gain, res[:, b, cols], ALU.mult, ALU.add,
                                             accum_out=st[:, i:i + 1]).then_inc(ln_chain, 1)
                dve.wait_ge(ln_chain, X * 4 + 2)
                dve.tensor_scalar(st[:, 2:3], st[:, 0:1], st[:, 1:2], -1.0 / D, ALU.add, ALU.mult
                                  ).then_inc(ln_chain, 1)

            def ln_gain(l, n, b):
                X = l * 12 + (4 * n + b)
                y, st = yb[:, b % 2], lns[:, b % 2]
                dve.wait_ge(ln_chain, X * 4 + 3)
                if b == 0:
                    dve.wait_ge(gb_landed, l * 48 + (16 * n + 16))
                else:
                    dve.wait_ge(y_ready, X + C_Y)
                dve.scalar_tensor_tensor(yg[:], y, st[:, 2:3], gb[:, 0], ALU.add, ALU.mult).then_inc(ln_chain, 1)

            def ln_out(l, n, b):
                X = l * 12 + (4 * n + b)
                dve.wait_ge(ln_chain, X * 4 + 4)
                dve.wait_ge(rstd_ready, X + 1)
                dve.scalar_tensor_tensor(res[:, b], yg[:], lns[:, b % 2, 5:6], gb[:, 1], ALU.mult, ALU.add
                                         ).then_inc(y_ready, 1)

            def xt(l, n, b):
                for i in range(2):
                    dve.wait_ge(xhi_ready, l * 24 + (KD + 8 * n + 2 * b + i + 1))
                    at = (slice(None), slice(4 * i, 4 * i + 4), slice(b * P, (b + 1) * P))
                    dve.tensor_tensor(x_lo[at], bank[2 * b + i][:].rearrange("p (k n) -> p k n", k=4),
                                      f32(x_hi[at]), ALU.subtract).then_inc(xlo_ready, 1)

            def tail(l, n, q, s):
                for b in range(2):
                    ln_sums(l, n, b)
                    ln_gain(l, n, b)
                    ln_out(l, n, b)
                xt(l, n, 0)
                ln_sums(l, n, 2)
                ln_gain(l, n, 2)
                xt(l, n, 1)
                split(*adv(q, s, 0))
                ln_out(l, n, 2)
                ln_sums(l, n, 3)
                split(*adv(q, s, 1))
                ln_gain(l, n, 3)
                ln_out(l, n, 3)

            def resume(l, n, q, s):
                split(*adv(q, s, 2))
                xt(l, n, 2)
                xt(l, n, 3)

            def softplus(l):
                cols = bass.ds(l * KR, KR)
                lam = pr[:, bass.ds(l * NPAR + PC["lam"], KR)]
                steps = [0]

                def link(ins):
                    steps[0] += 1
                    ins.then_inc(lam_dve, 1)
                    dve.wait_ge(lam_dve, l * N_LAM + steps[0])

                dve.wait_ge(par_landed, 16)
                link(dve.scalar_tensor_tensor(lt[:, 0], lam, -1.0, lam, ALU.mult, ALU.max))
                dve.wait_ge(lam_act, l + 1)
                link(dve.tensor_scalar(lt[:, 2], lt[:, 1], 2.0, None, ALU.add))
                settle(dve)
                link(dve.reciprocal(lt[:, 2], lt[:, 2]))
                link(dve.tensor_tensor(lt[:, 1], lt[:, 1], lt[:, 2], ALU.mult))
                link(dve.tensor_tensor(lt[:, 2], lt[:, 1], lt[:, 1], ALU.mult))
                link(dve.tensor_scalar(lt[:, 3], lt[:, 2], 1.0 / 15.0, None, ALU.mult))
                for k in (13, 11, 9, 7, 5, 3):
                    link(dve.scalar_tensor_tensor(lt[:, 3], lt[:, 3], 1.0 / k, lt[:, 2], ALU.add, ALU.mult))
                link(dve.scalar_tensor_tensor(lt[:, 3], lt[:, 3], 1.0, lt[:, 1], ALU.add, ALU.mult))
                link(dve.tensor_scalar(lt[:, 0], lam, -1.0, 0.0, ALU.mult, ALU.max))
                link(dve.scalar_tensor_tensor(lt[:, 0], lt[:, 3], 2.0, lt[:, 0], ALU.mult, ALU.add))
                link(dve.tensor_scalar(sp8[:, 0, cols], lt[:, 0], 8.0, None, ALU.mult))
                link(dve.tensor_scalar(sp8[:, 1, cols], lt[:, 0], -8.0, None, ALU.mult))
                assert steps[0] == N_LAM

            def ffn(l, f):
                q, s = q0(l, U_FFN[f])
                N0 = l * (2 * KF + KD) + f * (KF + KD)

                def pair(q, s, t, down, bk):
                    T = l * (2 * KF) + (f * KF + t)
                    for i in range(2):
                        split(*adv(q, s, AHEAD + i))
                        if down[i] is not None:
                            asplit(adv(q, s, AHEAD + i)[1], h, down[i], N0 + down[i])
                    dve.wait_ge(silu_done, T + 1)
                    dve.wait_ge(unit_done, U(*adv(q, s, 1)) + (RING + 1))
                    dve.tensor_tensor(one(h, t), bank[bk + 1][:], sg[:, 0], ALU.mult).then_inc(hmul_done, 1)

                with dve.Fori(0, KF // 2 - 1) as it:
                    pair(*adv(q + it, s, 0), it * 2, (None, None), 0)
                    pair(*adv(q + it, s, 2), it * 2 + 1, (None, None), 2)
                if f == 0:
                    softplus(l)
                pair(*adv(q, s, 2 * KF - 4), KF - 2, (None, 0), 0)
                pair(*adv(q, s, 2 * KF - 2), KF - 1, (1, 2), 2)
                qd, sd = adv(q, s, 2 * KF)
                for k in (0, 1):
                    split(*adv(qd, sd, k + AHEAD))
                    asplit(adv(qd, sd, k + AHEAD)[1], h, k + AHEAD, N0 + (k + AHEAD))
                with dve.Fori(0, 4) as it:
                    for i in range(4):
                        split(*adv(qd + it, sd, 2 + i + AHEAD))
                        k = it * 4 + (2 + i + AHEAD)
                        asplit(adv(qd, sd, 2 + i + AHEAD)[1], h, k, N0 + k)
                split(*adv(qd, sd, 18 + AHEAD))
                asplit(adv(qd, sd, 18 + AHEAD)[1], h, 18 + AHEAD, N0 + (18 + AHEAD))
                tail(l, 2 * f, *adv(qd, sd, KF))
                if f == 0:
                    resume(l, 0, *adv(qd, sd, KF))

            def taps(l, rel):
                for n in range(TAPS_BY[rel - 1], TAPS_BY[rel]):
                    c, k = n // VTAPS, n % VTAPS + 2
                    T = l * (KD * VTAPS) + n
                    acc = accs[c][k % 2]
                    if k < 4:
                        dve.wait_ge(init_done, l * (2 * KD) + (2 * c + k - 1))
                    else:
                        dve.wait_ge(tap_done, T - 1)
                    dve.scalar_tensor_tensor(acc, cpad[:, c, k:k + S], col("cw", l, c * TAPS + k), acc,
                                             ALU.mult, ALU.add).then_inc(tap_done, 1)
                    if k == TAPS - 1:
                        dve.wait_ge(tap_done, T + 1)
                        dve.tensor_tensor(conv_out(c), *accs[c], ALU.add).then_inc(conv_done, 1)

            def gn_center(l, g):
                dve.wait_ge(mean_done, l * KD + g + 1)
                dve.tensor_tensor(conv_out(g), conv_out(g), bank[6][:], ALU.subtract).then_inc(xc_done, 1)

            def gn_scale(l, g):
                dve.wait_ge(grs_done, l * KD + g + 1)
                dve.tensor_tensor(conv_out(g), conv_out(g), grs, ALU.mult).then_inc(gy_done, 1)

            dve.memset(epsb[:], EPS).then_inc(eps_ready, 1)
            xt(0, -1, 0)
            split(0, 0)
            xt(0, -1, 1)
            split(0, 1)
            dve.wait_ge(eps_ready, 1)

            with dve.Fori(0, L) as l:
                resume(l, -1, *q0(l, 0))
                ffn(l, 0)
                dve.wait_ge(y_ready, l * 12 + (NB + C_Y))
                settle(dve)
                dve.memset(cpad[:, :, 0:TAPS - 1], 0.0).then_inc(pads_ready, 1)
                dve.memset(rxp[:, :, 0:RTAPS - 1], 0.0).then_inc(pads_ready, 1)

                def ahead(rel):
                    split(*q0(l, rel + AHEAD), unit_cols(rel + AHEAD))

                def c_gated(j):
                    dve.wait_ge(csig_done, l * KD + (j + 1))
                    dve.scalar_tensor_tensor(conv_out(j), bank[2 * (j % 2)][:], col("b_c", l, 2 * j), sgc,
                                             ALU.add, ALU.mult).then_inc(cmul_done, 1)

                for i in range(2 * KD):
                    ahead(U_C + i)
                    if i % 2 == 0 and i:
                        c_gated(i // 2 - 1)
                    taps(l, U_C + i)

                def norm_steps(i, g):
                    if i % 4 == 1:
                        gn_center(l, g)
                    if i % 4 == 3:
                        gn_scale(l, g)

                for i in range(KR):
                    ahead(U_RG + i)
                    if i == 0:
                        c_gated(KD - 1)
                    if i % 4 == 1:
                        norm_steps(i, i // 4)
                    taps(l, U_RG + i)
                    if i % 4 == 3:
                        norm_steps(i, i // 4)

                def rconv(j):
                    n = l * (KR * 3) + 3 * j
                    dve.wait_ge(rx_done, l * KR + (j + 1 + C_RX))
                    if j >= 5:
                        dve.wait_ge(rclo_ready, l * KR + (j - 4))
                        dve.wait_ge(rv_done, l * (KR * 2) + (2 * ((j - 5) // 2 * 2) + (j - 5) % 2 + 1))
                    w = lambda k: col("rw", l, RTAPS * j + k)
                    src = lambda k: rxp[:, j % 2, k:k + S]
                    dst = rcf[j % 5]
                    dve.tensor_scalar(dst, src(0), w(0), col("rb", l, j), ALU.mult, ALU.add).then_inc(rtap_done, 1)
                    for k in range(1, RTAPS):
                        dve.wait_ge(rtap_done, n + k)
                        dve.scalar_tensor_tensor(dst, src(k), w(k), dst, ALU.mult, ALU.add
                                                 ).then_inc(rtap_done if k < RTAPS - 1 else rc_done, 1)

                def rc_lo(j):
                    dve.wait_ge(rchi_ready, l * KR + (j + 1))
                    dve.tensor_tensor(a_lo[:, j % 4], rcf[j % 5], f32(a_hi[:, j % 4]), ALU.subtract
                                      ).then_inc(rclo_ready, 1)

                def r_inputs(js):
                    for j in js:
                        r, i, a, v = RT[j % 2]
                        dve.wait_ge(ra_done, l * (KR * 5) + (5 * js[0] + 2 * (j - js[0]) + 2 + C_RA * 5))
                        dve.tensor_tensor(i, i, rcf[j % 5], ALU.mult).then_inc(rv_done, 1)

                def r_squares(js):
                    for m, j in enumerate(js):
                        r, i, a, v = RT[j % 2]
                        dve.wait_ge(ra_done, l * (KR * 5) + (5 * js[0] + 2 * len(js) + 3 * (m + 1) + C_RA * 5))
                        dve.scalar_tensor_tensor(v, v, 1.0, r, ALU.add, ALU.mult).then_inc(rv_done, 1)

                def r_scans(js):
                    n = l * (KR * 2) + 2 * js[0]
                    for j in js:
                        r, i, a, v = RT[j % 2]
                        dve.wait_ge(rs_done, l * KR + (j + 1))
                        dve.scalar_tensor_tensor(v, v, SQ_UP ** -0.5, i, ALU.mult, ALU.mult).then_inc(ru_done, 1)
                    for m, j in enumerate(js):
                        r, i, a, v = RT[j % 2]
                        dve.wait_ge(ru_done, n + (m + 1))
                        dve.tensor_tensor_scan(hgm[:, j], a, v, 0.0, ALU.mult, ALU.add).then_inc(ru_done, 1)
                    for m, j in enumerate(js):
                        dve.wait_ge(ru_done, n + (len(js) + m + 1))
                        dve.wait_ge(gelu_done, l * KR + (j + 1 + C_GELU))
                        dve.tensor_tensor(hgm[:, j], hgm[:, j], gates[:, j], ALU.mult).then_inc(hg_done, 1)

                rel = U_R
                for i in range(3):
                    ahead(rel + i)
                    if i:
                        rconv(i - 1)
                    if i == 1:
                        gn_scale(l, 2)
                    if i == 2:
                        rc_lo(0)
                    taps(l, rel + i)
                rel += 3
                for p in range(0, KR - 1, 2):
                    old = [p - 2, p - 1] if p else []
                    for i in range(6):
                        ahead(rel + i)
                        if i == 0 and p == 0:
                            rc_lo(1)
                        if i == 0:
                            rconv(p + 2)
                            r_inputs(old)
                        if i == 1:
                            rc_lo(p + 2)
                            if p + 3 < KR:
                                rconv(p + 3)
                        if i == 2 and old:
                            r_squares(old)
                        if i == 3:
                            if p + 3 < KR:
                                rc_lo(p + 3)
                            if old:
                                r_scans(old)
                        taps(l, rel + i)
                    rel += 6
                old, last = [KR - 3, KR - 2], [KR - 1]
                for i in range(3):
                    ahead(rel + i)
                    (r_inputs, r_squares, r_scans)[i](old)
                    taps(l, rel + i)

                def hg_lo(j, n):
                    dve.wait_ge(hs_hi, l * KR + (n + 1))
                    dve.tensor_tensor(hg_pair(j)[1], hgm[:, j], f32(hg_pair(j)[0]), ALU.subtract).then_inc(hs_lo, 1)

                def c_lo(j):
                    dve.wait_ge(cs_hi, l * KD + (j + 1))
                    dve.tensor_tensor(c_pair(j)[1], conv_out(j), f32(c_pair(j)[0]), ALU.subtract).then_inc(cs_lo, 1)

                for i in range(G_EARLY, 2 * KD):
                    ahead(g_rel(i))
                    if i < 6:
                        (r_inputs, r_squares, r_scans)[i - 3](last)
                    if i > 8 and i % 4 == 1:
                        norm_steps(i, i // 4 + 1)
                    if i == 12:
                        for m, j in enumerate(HG_SLOT):
                            hg_lo(j, m)
                    taps(l, g_rel(i))
                    if i > 8 and i % 4 == 3:
                        norm_steps(i, i // 4 + 1)

                def mix_r(f):
                    dve.wait_ge(unit_done, done(l, U_YR + 2 * f + 1))
                    dve.wait_ge(gate_done, l * (2 * KD) + (2 * f + 2 + C_GATE))
                    g = gates[:, 2 * f + 1]
                    dve.tensor_tensor(g, bank[(2, 0)[f % 2]][:], g, ALU.mult).then_inc(mr_done, 1)

                for m in range(KR - len(HG_SLOT)):
                    hg_lo(m, len(HG_SLOT) + m)
                for i in range(2 * KD):
                    ahead(U_YR + i)
                    if i % 2 == 0 and i:
                        mix_r(i // 2 - 1)
                    if i % 4 == 3 and i < 12:
                        gn_center(l, i // 4 + 5)
                    taps(l, U_YR + i)
                    if i % 4 == 1 and i > 4:
                        gn_scale(l, i // 4 + 4)
                    if i == 15:
                        for j in C_SLOT:
                            c_lo(j)

                def mix(f):
                    dve.wait_ge(unit_done, done(l, U_YC + f))
                    g = gates[:, 2 * f]
                    dve.tensor_tensor(g, bank[(1, 3)[f % 2]][:], g, ALU.mult).then_inc(mc_done, 1)
                    dve.wait_ge(mc_done, l * KD + (f + 1))
                    dve.wait_ge(mr_done, l * KD + (f + 1 + C_MR))
                    dve.tensor_tensor(hgm[:, f], g, gates[:, 2 * f + 1], ALU.add).then_inc(m_done, 1)

                mix_r(KD - 1)
                for j in range(3, KD):
                    c_lo(j)
                for i in range(KD):
                    ahead(U_YC + i)
                    if i:
                        mix(i - 1)
                N0 = l * (2 * KF + KD) + KF
                asplit(q0(l, U_O)[1], hgm, 0, N0)
                mix(KD - 1)

                for k in range(1, AHEAD):
                    asplit(q0(l, U_O + k)[1], hgm, k, N0 + k)
                for k in range(AHEAD, KD):
                    split(*q0(l, U_O + k))
                    asplit(q0(l, U_O + k)[1], hgm, k, N0 + k)
                tail(l, 1, *q0(l, U_O + KD))
                resume(l, 1, *q0(l, U_O + KD))

                ffn(l, 1)

        @block.tensor
        def _(pe):
            pe.sem_inc(unit_done, RING)

            def products(dst, tiles, first, last):
                for i, (sh, sl, mh, ml) in enumerate(tiles):
                    f, z = first and i == 0, last and i == len(tiles) - 1
                    pe.matmul(dst, sh, mh, start=f, stop=False)
                    pe.matmul(dst, sh, ml, start=False, stop=False)
                    ins = pe.matmul(dst, sl, mh, start=False, stop=z)
                return ins

            def wtile(s, i):
                return w_hi[:, s, i * P:(i + 1) * P], w_lo[:, s, i * P:(i + 1) * P]

            def in_part(s, dst, tok):
                return products(dst[:, tok], [(*wtile(s, k), x_hi[:, k, tok], x_lo[:, k, tok]) for k in range(KD)],
                                True, True)

            def in_unit(q, s, dst):
                pe.wait_ge(lo_ready, U(q, s) + (RING + 1))
                in_part(s, dst, slice(0, S)).then_inc(unit_done, 1)

            def out_unit(q, s, n, b, first, last):
                for i in range(2):
                    ins = products(bank[2 * b + i][:], [(a_hi[:, s, b * P:(b + 1) * P], a_lo[:, s, b * P:(b + 1) * P],
                                                         w_hi[:, s, i * S:i * S + S], w_lo[:, s, i * S:i * S + S])],
                                   first, last)
                return ins

            def xpose(l, n, b):
                pe.wait_ge(y_ready, l * 12 + (4 * n + b + 1 + C_Y))
                for i in range(2):
                    for k in range(4):
                        ins = pe.transpose(bank[2 * b + i][:, k * P:(k + 1) * P],
                                           res[:, b, (4 * i + k) * P:(4 * i + k + 1) * P], ident[:])
                    ins.then_inc(xpose_done, 1)

            def first_units(l, n, q, s):
                pe.wait_ge(xlo_ready, l * 24 + (8 * n + KD + 4))
                for half in range(2):
                    for i in range(3):
                        qq, ss = adv(q, s, i)
                        if half == 0:
                            pe.wait_ge(lo_ready, U(qq, ss) + (RING + 1))
                        ins = in_part(ss, bank[i], HALVES[half])
                        if half == 0 and i < 2:
                            xpose(l, n, 2 + i)
                        if half == 1:
                            ins.then_inc(unit_done, 1)
                    if half == 0:
                        pe.wait_ge(xlo_ready, l * 24 + (8 * n + KD + 8))

            def projection(l, n, rel, N0, K, banks01_free):
                q, s = q0(l, rel)

                def ready(k, q, s):
                    pe.wait_ge(lo_ready, U(q, s) + (RING + 1))
                    pe.wait_ge(alo_ready, N0 + k + 1)

                def whole(k, q, s, first=False):
                    ready(k, q, s)
                    for b in (2, 3, 0, 1):
                        if first and b == 0:
                            banks01_free()
                        ins = out_unit(q, s, N0, b, first, False)
                    ins.then_inc(unit_done, 1)

                whole(0, q, s, True)
                lead = (K - 4) % 4 or 4
                for k in range(1, lead):
                    whole(k, *adv(q, s, k))
                if K - 4 - lead:
                    with pe.Fori(0, (K - 4 - lead) // 4) as it:
                        for i in range(4):
                            whole(it * 4 + (lead + i), *adv(q + it, s, lead + i))
                for b in range(NB):
                    for k in range(K - 4, K):
                        qq, ss = adv(q, s, k)
                        if b == 0:
                            ready(k, qq, ss)
                        ins = out_unit(qq, ss, N0, b, False, k == K - 1)
                        if b == NB - 1:
                            ins.then_inc(unit_done, 1)
                    if b < NB - 1:
                        ins.then_inc(blk_done, 1)
                    if 0 < b < NB - 1:
                        xpose(l, n, b - 1)
                if n < 2:
                    first_units(l, n, *adv(q, s, K))

            def ffn(l, f):
                q, s = q0(l, U_FFN[f])

                def pair(it, t, first=0):
                    pe.wait_ge(hmul_done, l * (2 * KF) + it * 2 + (f * KF + t + 1))
                    for i in range(first, 2):
                        in_unit(*adv(q + it, s, 2 * t + i), bank[2 * t + i])

                pair(0, 1, 1)
                with pe.Fori(1, KF // 2) as it:
                    pair(it, 0)
                    pair(it, 1)
                projection(l, 2 * f, U_FFN[f] + 2 * KF, l * (2 * KF + KD) + f * (KF + KD), KF,
                           lambda: pe.wait_ge(hmul_done, l * (2 * KF) + (f * KF + KF + C_HMUL)))

            def gn_mean(l, g):
                pe.wait_ge(conv_done, l * KD + g + 1)
                pe.matmul(bank[6][:], avg[:], conv_out(g), start=True, stop=True).then_inc(mean_done, 1)

            def gn_var(l, g):
                pe.wait_ge(sq_done, l * KD + g + 1)
                pe.matmul(bank[7][:], avg[:], gsq, start=True, stop=True).then_inc(var_done, 1)

            pe.wait_ge(consts, 4)
            xpose(0, -1, 0)
            xpose(0, -1, 1)
            with pe.Fori(0, L) as l:
                first_units(l, -1, *q0(l, 0))
                ffn(l, 0)

                def c_group(it, first):
                    q, s = q0(l, U_C)
                    for i in range(first, 4):
                        if i % 2 == 0 or i == first:
                            pe.wait_ge(cmul_done, l * KD + it * 2 + (i // 2 + 1))
                        in_unit(*adv(q + it, s, i), bank[i])

                c_group(0, 3)
                with pe.Fori(1, 4) as it:
                    c_group(it, 0)

                def rg_group(it, n):
                    q, s = q0(l, U_RG)
                    for i in range(n):
                        if i % 2 == 0:
                            pe.wait_ge(cmul_done, l * KD + (KD - 1 + i // 2 + C_CMUL))
                        pe.wait_ge(gelu_done, l * KR + it * 4 + (i + 1))
                        in_unit(*adv(q + it, s, i), bank[i])
                        if i == 0:
                            gn_mean(l, it)
                        if i == 2:
                            gn_var(l, it)

                with pe.Fori(0, 2) as it:
                    rg_group(it, 4)
                rg_group(2, 3)

                for i, (kind, j) in enumerate(R_UNITS):
                    q, s = q0(l, U_R + i)
                    if kind == "rx":
                        pe.wait_ge(rx_done, l * KR + (j + 1))
                        in_unit(q, s, bank[4 + j % 2])
                        continue
                    if kind == "g":
                        if j < 2:
                            pe.wait_ge(rx_done, l * KR + (KR - 1 + j + C_RX))
                        if j == 2:
                            pe.wait_ge(xc_done, l * KD + 3)
                        in_unit(q, s, g_bank(j))
                        continue
                    if kind == "bda":
                        if j < 2:
                            pe.wait_ge(gelu_done, l * KR + (KR + C_GELU))
                        else:
                            pe.wait_ge(ra_done, l * (KR * 5) + (5 * (j // 2 * 2 - 2) + 2 * (j % 2 + 1) + C_RA * 5))
                        pe.wait_ge(rclo_ready, l * KR + min(j + 2, KR))
                    pe.wait_ge(lo_ready, U(q, s) + (RING + 1))
                    near = [t for t in (j - 1, j, j + 1) if 0 <= t < KR]
                    products(bank[(0 if kind == "bda" else 2) + j % 2][:],
                             [(*wtile(s, t - j + 1), a_hi[:, t % 4], a_lo[:, t % 4]) for t in near], True, True
                             ).then_inc(unit_done, 1)

                def g_group(it, stats=True):
                    q, s = q0(l, U_G + 4 - G_EARLY)
                    for i in range(4):
                        if i == 2:
                            pe.wait_ge(ra_done, l * (KR * 5) + (5 * (KR - 3) + 4 + C_RA * 5))
                        pe.wait_ge(gate_done, l * (2 * KD) + it * 4 + (i + 5))
                        in_unit(*adv(q + it, s, i), g_bank(i + 4))
                        if i == 0 and stats:
                            gn_mean(l, it + 2)
                        if i == 2 and stats:
                            gn_var(l, it + 2)

                pe.wait_ge(gln_done, l * KD + 3)
                in_unit(*q0(l, U_G), g_bank(3))
                g_group(0, False)
                with pe.Fori(1, 3) as it:
                    g_group(it)

                def yr_tile(it, ff, first=False, stats=True):
                    q, s = q0(l, U_YR)
                    pe.wait_ge(mr_done, l * KD + it * 2 + (ff + 1))
                    for i, (k0, k1) in enumerate(YR_SPLIT):
                        qq, ss = adv(q + it, s, 2 * ff + i)
                        pe.wait_ge(lo_ready, U(qq, ss) + (RING + 1))
                        for k in range(k0, k1):
                            if first:
                                pe.wait_ge(hs_lo, l * KR + (k + 1))
                            ins = products(bank[(2, 0)[ff]][:], [(*wtile(ss, k - k0), *hg_pair(YR_ORDER[k]))],
                                           k == 0, k == KR - 1)
                        ins.then_inc(unit_done, 1)
                        if i == 0 and stats and ff == 0:
                            gn_var(l, it + 4)
                        if i == 0 and stats and ff == 1:
                            gn_mean(l, it + 5)

                pe.wait_ge(ra_done, l * (KR * 5) + (5 * (KR - 1) + 2 + C_RA * 5))
                yr_tile(0, 0, True, False)
                yr_tile(0, 1)
                with pe.Fori(1, KD // 2 - 1) as it:
                    yr_tile(it, 0)
                    yr_tile(it, 1)
                yr_tile(KD // 2 - 1, 0)
                yr_tile(KD // 2 - 1, 1, False, False)

                def yc_tile(q, s, i, n, first=False):
                    pe.wait_ge(m_done, n)
                    qq, ss = adv(q, s, i)
                    pe.wait_ge(lo_ready, U(qq, ss) + (RING + 1))
                    for k in range(KD):
                        if first:
                            pe.wait_ge(cs_lo, l * KD + (k + 1))
                        ins = products(bank[(1, 3)[i % 2]][:], [(*wtile(ss, k), *c_pair(k))], k == 0, k == KD - 1)
                    ins.then_inc(unit_done, 1)

                q, s = q0(l, U_YC)
                pe.wait_ge(gate_done, l * (2 * KD) + (2 * KD + C_GATE))
                for i in range(4):
                    yc_tile(q, s, i, l * KD + (i + 1), i == 0)
                for i in range(4):
                    yc_tile(q + 1, s, i, l * KD + (i + 5))

                projection(l, 1, U_O, l * (2 * KF + KD) + KF, KD,
                           lambda: pe.wait_ge(m_done, l * KD + (KD + C_M)))

                ffn(l, 1)


def _units(np, i):
    W = np.zeros((L, UPL, P, UW), np.float32)

    def tiles(w, cols):
        K = w.shape[0] // P
        return [w[:, c:c + P].reshape(K, P, P).transpose(1, 0, 2).reshape(P, K * P) for c in cols]

    for l in range(L):
        for f, n in enumerate(("ffn1", "ffn2")):
            gu, down = i[f"{n}_w_gu"][l], i[f"{n}_w_down"][l]
            b = U_FFN[f]
            for t in range(KF):
                W[l, b + 2 * t], W[l, b + 2 * t + 1] = tiles(gu, (t * P, DFF + t * P))
            W[l, b + 2 * KF:b + 3 * KF] = down.reshape(KF, P, D)
        w = i["mix_w_in"][l]
        oc, og = 0, D
        orx, org = 2 * D, 2 * D + DRNN
        ogc, ogr = 2 * D + 2 * DRNN, 3 * D + 2 * DRNN
        gates = []
        for j in range(KD):
            W[l, U_C + 2 * j], W[l, U_C + 2 * j + 1] = tiles(w, (oc + j * P, og + j * P))
            gates += tiles(w, (ogc + j * P, ogr + j * P))
        W[l, U_G:U_YR] = gates[G_EARLY:]
        for j in range(KR):
            W[l, U_RG + j] = tiles(w, (org + j * P,))[0]
        band = {}
        for kind, name in (("bda", "rnn_w_a"), ("bdx", "rnn_w_x")):
            m = np.zeros((DRNN, DRNN), np.float32)
            for b in range(DRNN // RB):
                m[b * RB:(b + 1) * RB, b * RB:(b + 1) * RB] = i[name][l, b]
            band[kind] = m
        for n, (kind, j) in enumerate(R_UNITS):
            if kind == "g":
                W[l, U_R + n] = gates[j]
                continue
            if kind == "rx":
                W[l, U_R + n] = tiles(w, (orx + j * P,))[0]
                continue
            for t in (j - 1, j, j + 1):
                if 0 <= t < KR:
                    W[l, U_R + n, :, (t - j + 1) * P:(t - j + 2) * P] = \
                        band[kind][t * P:(t + 1) * P, j * P:(j + 1) * P]
        for f in range(KD):
            t = tiles(i["rnn_w_proj"][l], (f * P,))[0].reshape(P, KR, P)[:, YR_ORDER].reshape(P, KR * P)
            for n, (k0, k1) in enumerate(YR_SPLIT):
                W[l, U_YR + 2 * f + n, :, 0:(k1 - k0) * P] = t[:, k0 * P:k1 * P]
            W[l, U_YC + f] = tiles(i["conv_w_proj"][l], (f * P,))[0]
        W[l, U_O:U_O + KD] = i["mix_w_out"][l].reshape(KD, P, D)
    return W.reshape(L * UPL, P, UW)


def _params(np, i):
    A = np.zeros((P, L, NPAR), np.float32)

    def put(name, l, v, at=0, step=1):
        v = v.reshape(v.shape[0] // P, P, -1).transpose(1, 0, 2)
        n = v.shape[1] * v.shape[2]
        A[:, l, PC[name] + at:PC[name] + at + step * (n - 1) + 1:step] = v.reshape(P, n)

    for l in range(L):
        b = i["mix_b_in"][l]
        put("b_c", l, b[0:D], 0, 2)
        put("b_c", l, b[D:2 * D], 1, 2)
        o = 2 * D
        put("b_rx", l, b[o:o + DRNN])
        put("b_rg", l, b[o + DRNN:o + 2 * DRNN])
        o += 2 * DRNN
        put("b_g", l, b[o:o + D], 0, 2)
        put("b_g", l, b[o + D:o + 2 * D], 1, 2)
        put("cw", l, i["conv_dw_w"][l].T)
        put("cb", l, i["conv_dw_b"][l])
        put("gg", l, i["conv_gn_g"][l])
        put("gb", l, i["conv_gn_b"][l])
        put("rw", l, i["rnn_conv_w"][l].T)
        put("rb", l, i["rnn_conv_b"][l])
        put("ba", l, i["rnn_b_a"][l])
        put("bx", l, i["rnn_b_x"][l])
        put("lam", l, i["rnn_lambda"][l])
    return A.reshape(P, L * NPAR)


def kernel(**inputs):
    import numpy as np
    import concourse.bacc as bacc
    from concourse.bass_utils import run_bass_kernel_spmd

    i = {k: np.asarray(v) for k, v in inputs.items()}
    x = i["x"].reshape(S, D)
    lnp = np.empty((L * 3, P, 2, D), np.float32)
    for l in range(L):
        for n in range(3):
            lnp[3 * l + n, :, 0], lnp[3 * l + n, :, 1] = i[f"ln{n + 1}_g"][l], i[f"ln{n + 1}_b"][l]
    arrays = {
        "wst": _units(np, i),
        "xtok": np.ascontiguousarray(x),
        "par": _params(np, i),
        "lnp": lnp,
    }
    nc = bacc.Bacc("TRN2", target_bir_lowering=False, num_devices=1)
    args = [nc.dram_tensor(n, a.shape, F32, kind="ExternalInput").ap() for n, a in arrays.items()]
    out = nc.dram_tensor("out", (S, D), F32, kind="ExternalOutput").ap()
    trunk(nc, *args, out)
    r = run_bass_kernel_spmd(nc, [arrays], core_ids=[0])
    return r.results[0]["out"].reshape(1, S, D)
```
